# Optimizing a Trainium2 kernel written in Bass

```python
import math
import jax, jax.numpy as jnp
from jax import lax
import numpy as np

D_MODEL = 1024
BATCH = 1
SEQ = 128
DEPTH = 1
DEC_BATCH = 1
DEC_SEQ = 512
PAST_LEN = 128

GRID_W = 64
Q_BLOCK = 128
ROPE_THETA = 10000.0
LN_EPS = 1e-5
A_HEADS = 8
A_HEAD_DIM = 64
A_V_DIM = 2 * A_HEAD_DIM
B_HEADS = 16
B_KV_HEADS = 4
B_HEAD_DIM = 64
A_QK_W = A_HEADS * 2 * A_HEAD_DIM
A_V_W = A_HEADS * A_V_DIM
B_Q_W = B_HEADS * B_HEAD_DIM
B_KV_W = B_KV_HEADS * B_HEAD_DIM
IN_SPLITS = (A_QK_W, A_QK_W, A_V_W, B_Q_W, B_KV_W, B_KV_W, D_MODEL, D_MODEL)
IN_W = sum(IN_SPLITS)
IN_OFFSETS = [sum(IN_SPLITS[:i + 1]) for i in range(len(IN_SPLITS) - 1)]
N_GROUPS = 4
EXPERTS_PER_GROUP = 4
N_EXPERTS = N_GROUPS * EXPERTS_PER_GROUP
TOP_K_FINE = 2
EXPERT_FF = 512
DEEPNORM_ALPHA = (2 * DEPTH) ** 0.25
DEEPNORM_BETA = (8 * DEPTH) ** -0.25

kernel_name = "hybrid_diffattn_gqa_hiermoe_prefix_ctx_step"

def ln_plain(x):
    xf = x.astype(jnp.float32)
    mu = jnp.mean(xf, -1, keepdims=True)
    var = jnp.mean(jnp.square(xf - mu), -1, keepdims=True)
    return ((xf - mu) * lax.rsqrt(var + LN_EPS)).astype(x.dtype)

def ln_affine(x, g, b):
    xf = x.astype(jnp.float32)
    mu = jnp.mean(xf, -1, keepdims=True)
    var = jnp.mean(jnp.square(xf - mu), -1, keepdims=True)
    y = (xf - mu) * lax.rsqrt(var + LN_EPS) * g.astype(jnp.float32) + b.astype(jnp.float32)
    return y.astype(x.dtype)

def rms_norm(x, g):
    xf = x.astype(jnp.float32)
    y = xf * lax.rsqrt(jnp.mean(jnp.square(xf), -1, keepdims=True) + LN_EPS)
    return (y * g.astype(jnp.float32)).astype(x.dtype)

def axial_rope_tables(n_tokens, head_dim):
    n_rows = n_tokens // GRID_W
    rows = jnp.repeat(jnp.arange(n_rows, dtype=jnp.float32), GRID_W)
    cols = jnp.tile(jnp.arange(GRID_W, dtype=jnp.float32), n_rows)
    axis_dim = head_dim // 2
    freqs = ROPE_THETA ** (-jnp.arange(0, axis_dim, 2, dtype=jnp.float32) / axis_dim)
    ang = jnp.concatenate([rows[:, None] * freqs, cols[:, None] * freqs], -1)
    return jnp.cos(ang), jnp.sin(ang)

def apply_rope(x, cos, sin):
    xf = x.astype(jnp.float32).reshape(*x.shape[:-1], -1, 2)
    x1, x2 = xf[..., 0], xf[..., 1]
    c = cos[None, :, None, :]
    s = sin[None, :, None, :]
    out = jnp.stack([x1 * c - x2 * s, x1 * s + x2 * c], -1).reshape(x.shape)
    return out.astype(x.dtype)

def sweep_query_blocks(fn, q):
    b, s = q.shape[:2]
    nb = s // Q_BLOCK
    qb = jnp.moveaxis(q.reshape(b, nb, Q_BLOCK, *q.shape[2:]), 1, 0)
    out = lax.map(fn, qb)
    return jnp.moveaxis(out, 0, 1).reshape(b, s, out.shape[-1])

def diff_attention(q, k, v, lam, lambda_init, subln_g):
    scale = A_HEAD_DIM ** -0.5

    def block(qb):
        s = jnp.einsum('bqhnd,bkhnd->bhnqk', qb, k).astype(jnp.float32) * scale
        p = jax.nn.softmax(s, axis=-1)
        a = p[:, :, 0] - lam * p[:, :, 1]
        o = jnp.einsum('bhqk,bkhe->bqhe', a.astype(v.dtype), v)
        o = rms_norm(o, subln_g) * (1.0 - lambda_init)
        return o.reshape(o.shape[0], o.shape[1], -1)

    return sweep_query_blocks(block, q)

def gqa_attention(q, k, v):
    scale = B_HEAD_DIM ** -0.5
    n_rep = B_HEADS // B_KV_HEADS

    def block(qb):
        b, nq = qb.shape[:2]
        qg = qb.reshape(b, nq, B_KV_HEADS, n_rep, B_HEAD_DIM)
        s = jnp.einsum('bqhgd,bkhd->bhgqk', qg, k).astype(jnp.float32) * scale
        p = jax.nn.softmax(s, axis=-1)
        o = jnp.einsum('bhgqk,bkhd->bqhgd', p.astype(v.dtype), v)
        return o.reshape(b, nq, -1)

    return sweep_query_blocks(block, q)

def hier_moe(h, w_coarse, b_coarse, w_fine, b_fine, w_gate_up, w_down):
    b, s, d = h.shape
    t = h.reshape(-1, d)
    p_coarse = jax.nn.softmax((t @ w_coarse + b_coarse).astype(jnp.float32), axis=-1)
    p_grp, grp = lax.top_k(p_coarse, 1)
    grp_oh = jax.nn.one_hot(grp[:, 0], N_GROUPS, dtype=jnp.float32)
    fine_logits = (t @ w_fine + b_fine).astype(jnp.float32).reshape(-1, N_GROUPS, EXPERTS_PER_GROUP)
    fine_sel = jnp.einsum('tg,tge->te', grp_oh, fine_logits)
    p_fine = jax.nn.softmax(fine_sel, axis=-1)
    w_top, e_top = lax.top_k(p_fine, TOP_K_FINE)
    w_top = w_top / jnp.sum(w_top, -1, keepdims=True)
    within = jnp.einsum('tk,tke->te', w_top, jax.nn.one_hot(e_top, EXPERTS_PER_GROUP, dtype=jnp.float32))
    combine = ((p_grp * grp_oh)[:, :, None] * within[:, None, :]).reshape(-1, N_EXPERTS).astype(h.dtype)
    out = jnp.zeros_like(t)
    for e in range(N_EXPERTS):
        gg, uu = jnp.split(t @ w_gate_up[e], 2, axis=-1)
        out = out + combine[:, e:e + 1] * ((jax.nn.silu(gg) * uu) @ w_down[e])
    return out.reshape(b, s, d)

def trunk_layer(l, x, cond, ctx, rope_a, rope_b, p):
    b, s, _ = x.shape
    mod = jax.nn.silu(cond) @ p['w_ada'][l] + p['b_ada'][l]
    sh1, sc1, g1, sh2, sc2, g2 = jnp.split(mod[:, None, :], 6, axis=-1)

    h = ln_plain(x) * (1 + sc1) + sh1
    aq, ak, av, bq, bk, bv, ga, gb = jnp.split(h @ p['w_in'][l], IN_OFFSETS, axis=-1)
    aq = aq.reshape(b, s, A_HEADS, 2, A_HEAD_DIM)
    ak = ak.reshape(b, s, A_HEADS, 2, A_HEAD_DIM)
    av = av.reshape(b, s, A_HEADS, A_V_DIM)
    bq = rms_norm(bq.reshape(b, s, B_HEADS, B_HEAD_DIM), p['b_q_g'][l])
    bk = rms_norm(bk.reshape(b, s, B_KV_HEADS, B_HEAD_DIM), p['b_k_g'][l])
    bv = bv.reshape(b, s, B_KV_HEADS, B_HEAD_DIM)
    ctx_out = (ak, av, bk, bv)

    if rope_a is not None:
        aq = apply_rope(aq.reshape(b, s, 2 * A_HEADS, A_HEAD_DIM), *rope_a).reshape(aq.shape)
        ak = apply_rope(ak.reshape(b, s, 2 * A_HEADS, A_HEAD_DIM), *rope_a).reshape(ak.shape)
        bq = apply_rope(bq, *rope_b)
        bk = apply_rope(bk, *rope_b)

    if ctx is None:
        kA, vA, kB, vB = ak, av, bk, bv
    else:
        kA = jnp.concatenate([ak, ctx[0]], axis=1)
        vA = jnp.concatenate([av, ctx[1]], axis=1)
        kB = jnp.concatenate([bk, ctx[2]], axis=1)
        vB = jnp.concatenate([bv, ctx[3]], axis=1)

    lambda_init = 0.8 - 0.6 * math.exp(-0.3 * l)
    lam = (jnp.exp(jnp.sum(p['lambda_q1'][l].astype(jnp.float32) * p['lambda_k1'][l].astype(jnp.float32)))
           - jnp.exp(jnp.sum(p['lambda_q2'][l].astype(jnp.float32) * p['lambda_k2'][l].astype(jnp.float32)))
           + lambda_init)
    o_a = diff_attention(aq, kA, vA, lam, lambda_init, p['a_subln_g'][l])
    o_b = gqa_attention(bq, kB, vB)
    merged = jax.nn.sigmoid(ga) * (o_a @ p['w_br_a'][l]) + jax.nn.sigmoid(gb) * (o_b @ p['w_br_b'][l])
    x = ln_affine(DEEPNORM_ALPHA * x + g1 * (merged @ p['w_o'][l]), p['ln1_g'][l], p['ln1_b'][l])

    h = ln_plain(x) * (1 + sc2) + sh2
    y = hier_moe(h, p['w_coarse'][l], p['b_coarse'][l], p['w_fine'][l], p['b_fine'][l],
                 p['w_gate_up'][l], p['w_down'][l])
    x = ln_affine(DEEPNORM_ALPHA * x + g2 * y, p['ln2_g'][l], p['ln2_b'][l])
    return x, ctx_out

def setup_inputs(seed: int = 0) -> dict:
    key = jax.random.key(seed)
    ks = iter(jax.random.split(key, 40))
    f32 = jnp.float32

    def nrm(shape, scale=1.0):
        return jax.random.normal(next(ks), shape, f32) * scale

    D = D_MODEL
    return {
        'x_prompt': nrm((BATCH, SEQ, D)),
        'x_sample': nrm((DEC_BATCH, DEC_SEQ, D)),
        'cache_a_k': nrm((DEC_BATCH, DEPTH, PAST_LEN, A_HEADS, 2, A_HEAD_DIM)),
        'cache_a_v': nrm((DEC_BATCH, DEPTH, PAST_LEN, A_HEADS, A_V_DIM)),
        'cache_b_k': nrm((DEC_BATCH, DEPTH, PAST_LEN, B_KV_HEADS, B_HEAD_DIM)),
        'cache_b_v': nrm((DEC_BATCH, DEPTH, PAST_LEN, B_KV_HEADS, B_HEAD_DIM)),
        'c': nrm((DEC_BATCH, D)),
        'c_ctx': nrm((D,)),
        'w_ada': nrm((DEPTH, D, 6 * D), 0.5 * D ** -0.5),
        'b_ada': nrm((DEPTH, 6 * D), 0.02),
        'w_in': nrm((DEPTH, D, IN_W), D ** -0.5),
        'lambda_q1': nrm((DEPTH, A_HEAD_DIM), 0.1),
        'lambda_k1': nrm((DEPTH, A_HEAD_DIM), 0.1),
        'lambda_q2': nrm((DEPTH, A_HEAD_DIM), 0.1),
        'lambda_k2': nrm((DEPTH, A_HEAD_DIM), 0.1),
        'a_subln_g': 1.0 + nrm((DEPTH, A_V_DIM), 0.02),
        'b_q_g': 1.0 + nrm((DEPTH, B_HEAD_DIM), 0.02),
        'b_k_g': 1.0 + nrm((DEPTH, B_HEAD_DIM), 0.02),
        'w_br_a': nrm((DEPTH, A_V_W, D), A_V_W ** -0.5),
        'w_br_b': nrm((DEPTH, B_Q_W, D), B_Q_W ** -0.5),
        'w_o': nrm((DEPTH, D, D), DEEPNORM_BETA * D ** -0.5),
        'ln1_g': 1.0 + nrm((DEPTH, D), 0.02),
        'ln1_b': nrm((DEPTH, D), 0.02),
        'w_coarse': nrm((DEPTH, D, N_GROUPS), D ** -0.5),
        'b_coarse': nrm((DEPTH, N_GROUPS), 0.01),
        'w_fine': nrm((DEPTH, D, N_EXPERTS), D ** -0.5),
        'b_fine': nrm((DEPTH, N_EXPERTS), 0.01),
        'w_gate_up': nrm((DEPTH, N_EXPERTS, D, 2 * EXPERT_FF), D ** -0.5),
        'w_down': nrm((DEPTH, N_EXPERTS, EXPERT_FF, D), DEEPNORM_BETA * EXPERT_FF ** -0.5),
        'ln2_g': 1.0 + nrm((DEPTH, D), 0.02),
        'ln2_b': nrm((DEPTH, D), 0.02),
    }

def reference(x_prompt, x_sample, cache_a_k, cache_a_v, cache_b_k, cache_b_v, c, c_ctx,
              w_ada, b_ada, w_in, lambda_q1, lambda_k1, lambda_q2, lambda_k2, a_subln_g,
              b_q_g, b_k_g, w_br_a, w_br_b, w_o, ln1_g, ln1_b, w_coarse, b_coarse,
              w_fine, b_fine, w_gate_up, w_down, ln2_g, ln2_b):
    params = dict(w_ada=w_ada, b_ada=b_ada, w_in=w_in, lambda_q1=lambda_q1, lambda_k1=lambda_k1,
                  lambda_q2=lambda_q2, lambda_k2=lambda_k2, a_subln_g=a_subln_g, b_q_g=b_q_g,
                  b_k_g=b_k_g, w_br_a=w_br_a, w_br_b=w_br_b, w_o=w_o, ln1_g=ln1_g, ln1_b=ln1_b,
                  w_coarse=w_coarse, b_coarse=b_coarse, w_fine=w_fine, b_fine=b_fine,
                  w_gate_up=w_gate_up, w_down=w_down, ln2_g=ln2_g, ln2_b=ln2_b)

    cond_ctx = c_ctx[None, :]
    xp = x_prompt
    a_k_list, a_v_list, b_k_list, b_v_list = [], [], [], []
    for l in range(DEPTH):
        xp, (ak, av, bk, bv) = trunk_layer(l, xp, cond_ctx, None, None, None, params)
        a_k_list.append(ak)
        a_v_list.append(av)
        b_k_list.append(bk)
        b_v_list.append(bv)
    y_prompt = xp
    new_a_k = jnp.stack(a_k_list, axis=1)
    new_a_v = jnp.stack(a_v_list, axis=1)
    new_b_k = jnp.stack(b_k_list, axis=1)
    new_b_v = jnp.stack(b_v_list, axis=1)

    n_lat = x_sample.shape[1]
    rope_a = axial_rope_tables(n_lat, A_HEAD_DIM)
    rope_b = axial_rope_tables(n_lat, B_HEAD_DIM)
    xs = x_sample
    for l in range(DEPTH):
        ctx = (cache_a_k[:, l], cache_a_v[:, l], cache_b_k[:, l], cache_b_v[:, l])
        xs, _ = trunk_layer(l, xs, c, ctx, rope_a, rope_b, params)
    y_sample = xs

    return (y_prompt, y_sample, new_a_k, new_a_v, new_b_k, new_b_v)


_drawn_inputs = setup_inputs


def setup_inputs(seed=0):
    import zlib

    import numpy as np

    out = dict(_drawn_inputs(seed))
    spreads = {}
    factors = {'cache_a_k': 6.283,
     'cache_a_v': 5.671,
     'cache_b_k': 8.0,
     'cache_b_v': 8.0,
     'lambda_q1': 6.117,
     'lambda_k1': 8.0,
     'lambda_q2': 8.0,
     'lambda_k2': 8.0,
     'a_subln_g': 49.24,
     'b_q_g': 8.0,
     'b_k_g': 8.175,
     'ln1_g': 7.187,
     'ln1_b': 7.577,
     'b_coarse': 64.0,
     'b_fine': 64.0,
     'ln2_g': 8.458,
     'ln2_b': 8.122,
     'w_coarse': 3.874,
     'w_fine': 4.587,
     'w_gate_up': 3.384,
     'w_down': 3.372}
    for name, (base, spread) in spreads.items():
        noise = np.random.default_rng([zlib.crc32(name.encode()), seed]).standard_normal(out[name].shape)
        drawn = base * np.exp(spread * noise) if base else spread * noise
        out[name] = __import__('jax').numpy.asarray(drawn.astype(out[name].dtype))
    for name, factor in factors.items():
        out[name] = (out[name] * factor).astype(out[name].dtype)
    return out
```

```python
import math
from contextlib import ExitStack

import numpy as np

import concourse.bass as bass
from concourse import mybir

F32 = mybir.dt.float32
F32R = mybir.dt.float32r
I32 = mybir.dt.int32
U32 = mybir.dt.uint32
ACT = mybir.ActivationFunctionType
ALU = mybir.AluOpType
AX = mybir.AxisListType

P = 128
D = 1024
KD = D // P
N_LAT = 512
N_CTX = 128
TL = N_LAT // P
NT = TL + 1
PROMPT = TL
GRID_W = 64
HD = 64
A_HEADS = 8
B_HEADS = 16
B_KV = 4
REP = B_HEADS // B_KV
NE = 16
NG = 4
EPG = NE // NG
FF = 512
KF = FF // P
EPS = 1e-5
ALPHA = 2 ** 0.25
SCALE = HD ** -0.5
LAMBDA_INIT = 0.8 - 0.6 * math.exp(0.0)
CW = 512
NC_CH = 4
NKEY = N_LAT + N_CTX
KCOL = NKEY + P
RSQRT_MAGIC = 0x5F3759DF
MAPS_A = 2 * A_HEADS
PAIRS = 2 * P * NT
OVER = (PAIRS - NE) // P
TILES = NE + OVER + (NE + OVER) % 2
MORE = TILES - NE
T_TRI, T_ROW, T_PRI, T_PAIR, T_TILE, T_MORE = np.cumsum([0, NE * NE, NE, NG, MORE // 2, TILES]).tolist()
TAB_W = T_MORE + MORE
OFF = 3


def rsqrt(dve, link, y, v, half, shifted):
    link(dve.tensor_scalar(shifted, v.bitcast(I32), 1, None, ALU.logical_shift_right))
    link(dve.tensor_scalar(y.bitcast(I32), shifted, -1.0, float(RSQRT_MAGIC), ALU.mult, ALU.add))
    for _ in range(3):
        link(dve.tensor_tensor(half, y, y, ALU.mult))
        link(dve.scalar_tensor_tensor(half, half, -0.5, v, ALU.mult, ALU.mult))
        link(dve.scalar_tensor_tensor(y, half, 1.5, y, ALU.add, ALU.mult))


def chain(eng, sem):
    count = [0]

    def link(ins):
        count[0] += 1
        ins.then_inc(sem, 1)
        eng.wait_ge(sem, count[0])

    return link


def over(ap, n, shape):
    return ap.unsqueeze(n).to_broadcast(shape)


def hybrid_step(nc, t):
    with ExitStack() as ctx:
        def sb(name, shape, dt=F32, stack=ctx):
            return stack.enter_context(nc.sbuf_tensor(name, shape, dt))

        def sem(name):
            return ctx.enter_context(nc.semaphore(name))

        def dram(name, shape, dt=F32):
            return nc.dram_tensor(name, shape, dt, kind="Internal").ap()

        pair = [ctx.enter_context(nc.psum_tensor(f"psum_pair{i}", [P, 2 * CW], F32)) for i in range(4)]

        q_scr = dram("q_transposed", (MAPS_A + B_HEADS, P, NT * P))
        k_scr = dram("k_transposed", (MAPS_A + B_KV, P, KCOL))
        va_scr = dram("values_a", (P, NT, D))
        vb_scr = dram("values_b", (P, NT, B_KV * HD))
        gate_scr = dram("gate_tanh", (NT, P, 2 * D))
        mod_scr = dram("modulation", (2, 6 * D))
        o_scr = dram("attention_out", (NT, P, 2 * D))
        x1_scr = dram("x_after_ln1", (NT, P, D))
        slots_scr = dram("expert_rows", (TILES * P, D))

        ident = sb("identity", [P, P])
        pick_cols = sb("pick_cols", [5, 2])
        eps_row = sb("half_tiles", [P, 8])
        cond = sb("cond", [P, KD, 2])
        cond_t = sb("cond_tanh", [P, KD, 2])
        cond_hl = sb("cond_hi_lo", [P, KD, 4], F32R)
        mod_t = sb("mod_transposed", [P, 2 * KD, 2])
        w_raw = sb("w_raw", [P, NC_CH, 2, CW])
        w_hi = sb("w_hi", [P, 2, NC_CH, 2, CW], F32R)
        w_lo = sb("w_lo", [P, 2, NC_CH, 2, CW], F32R)

        raw_in = [sem(f"w_raw_in{c}") for c in range(NC_CH)]
        hi_done = sem("w_hi_done")
        lo_done = sem("w_lo_done")
        const_in = sem("const_in")
        x_in = sem("x_in")
        dve_link = sem("dve_link")
        act_link = sem("act_link")
        pj_ready = sem("proj_ready")
        pj_free = [sem(f"proj_free{i}") for i in range(4)]
        tr_ready = sem("turned_ready")
        tr_free = [sem(f"turned_free{i}") for i in range(2)]

        w_ada = t["w_ada"][0].rearrange("(k p) n -> p k n", p=P)
        w_in = t["w_in"][0].rearrange("(k p) n -> p k n", p=P)
        w_br = {"wa": t["w_br_a"][0].rearrange("(k p) n -> p k n", p=P),
                "wb": t["w_br_b"][0].rearrange("(k p) n -> p k n", p=P),
                "wo": t["w_o"][0].rearrange("(k p) n -> p k n", p=P)}
        blocks = [("ada", i) for i in range(4)]
        for i in range(13):
            blocks.append(("in", i))
            if i < 8:
                blocks.append(("ada", 4 + i))
        blocks += [("wa", 0), ("wb", 0), ("wa", 1), ("wb", 1), ("wo", 0), ("wo", 1)]
        NB = len(blocks)

        def block_chunk(b, c):
            kind, i = blocks[b]
            src = w_ada if kind == "ada" else w_in if kind == "in" else w_br[kind]
            return src[:, 2 * c:2 * c + 2, i * CW:(i + 1) * CW]

        KINDS = ["q", "q", "k", "k", "v", "v", "bq", "bq", "bkv", "g", "g", "g", "g"]
        units = []
        for b in range(4, NB - 6):
            kind, i = blocks[b]
            if kind == "ada":
                units.append(("ada", b, i, 0))
            else:
                if i == 2:
                    units += [("ck", None, 0, NT), ("ck", None, 1, NT), ("cbk", None, 0, NT)]
                units += [(KINDS[i], b, i, tt) for tt in range(NT)]
        units = [("ada", b, b, 0) for b in range(4)] + units
        N_EARLY = 4

        pj_no, n = {}, 0
        for i, (kind, b, _, _) in enumerate(units):
            if b is not None:
                pj_no[i] = n
                n += 1
        N_PJ = n
        last_no = {units[i][1]: pj_no[i] for i in sorted(pj_no)}
        GROUPS = {"q": 1, "k": 1, "bq": 1, "bkv": 1, "ck": 1, "cbk": 1, "ada": 1, "v": 0, "g": 0}
        tr_no, n = {}, 0
        for i in range(N_EARLY):
            tr_no[i] = [n]
            n += 1
        H_GROUP0 = n
        n += KD
        for i in range(N_EARLY, len(units)):
            tr_no[i] = list(range(n, n + GROUPS[units[i][0]]))
            n += GROUPS[units[i][0]]
        N_TR = n

        def key_col(tt):
            return {PROMPT: NKEY, NT: N_LAT}.get(tt, tt * P)

        def bank(n):
            return pair[(n % 4) // 2][:, (n % 2) * CW:(n % 2 + 1) * CW]

        def turned(n):
            return pair[2 + n % 2]

        def first_of_block(i):
            return units[i][1] is not None and (i == 0 or units[i - 1][1] != units[i][1]) and not (
                units[i][1] is not None and any(u[1] == units[i][1] for u in units[:i]))

        TST = 3
        tst_no, vst_no, pst_no, hl_no, ms_no = {}, {}, {}, {}, {}
        a = v = p = h = m = 0
        for i, (kind, b, ci, tt) in enumerate(units):
            if kind in ("q", "k", "bq", "bkv", "ck", "cbk"):
                tst_no[i] = list(range(a, a + GROUPS[kind]))
                a += GROUPS[kind]
                hl_no[i] = h
                h += 1
            if kind in ("v", "g", "bkv"):
                vst_no[i] = v
                v += 1
            if kind in ("k", "bkv") and tt == PROMPT:
                pst_no[i] = p
                p += 1
            if kind == "ada" and ci >= 4:
                ms_no[i] = m
                m += 1
        N_TST, N_VST, N_PST, N_MS = a, v, p, m
        hl_users = sorted(hl_no, key=lambda i: hl_no[i])

        tst_st = [sem(f"turned_stored{i}") for i in range(TST)]
        vst_st = [sem(f"values_stored{i}") for i in range(2)]
        pst_st = [sem(f"prompt_k_stored{i}") for i in range(2)]
        ms_st = [sem(f"mod_stored{i}") for i in range(2)]
        tst_sum, vst_sum = {}, {}
        count = [0] * TST
        for i in sorted(tst_no):
            for j in tst_no[i]:
                count[j % TST] += 16
                tst_sum[j] = count[j % TST]
        tst_total = list(count)
        count = [0] * 2
        for i in sorted(vst_no):
            j = vst_no[i]
            count[j % 2] += 32 if units[i][3] == PROMPT and units[i][0] != "g" else 16
            vst_sum[j] = count[j % 2]
        vst_total = list(count)

        stage5_in = [sem(f"bias_in{i}") for i in range(2)]
        cond_silu = sem("cond_silu")
        norm_done = sem("x_normed")
        aff_done = sem("h_affine")
        h_done = sem("h_split")
        sq_done = sem("squares_done")
        v_out = sem("v_staged")
        hl_done = sem("hl_done")
        pst_out = sem("prompt_k_staged")
        cache_in = sem("cache_in")

        s3a = ExitStack()
        NB_A = A_HEADS
        bundles = [(0, h) for h in range(A_HEADS)] + [(1, g) for g in range(B_KV)]
        qtb = [sb("q_bundle0", [P, REP, NT * P], F32R, s3a)]
        ktb = [sb("k_bundle0", [P, 2, 2, KCOL], F32R, s3a)]
        vb = [sb("v_bundle0", [P, NT + 1, P], F32, s3a)]
        s12 = ExitStack()
        h_hi = sb("h_hi", [P, KD, NT * P], F32R, s12)
        h_lo = sb("h_lo", [P, KD, NT * P], F32R, s12)
        stage5 = sb("mod_parts", [5, 2, CW], F32, s12)
        cache = sb("cache_k", [P, D + B_KV * HD], F32, s12)
        cosd = sb("rope_cos", [P, TL, HD], F32, s12)
        sind = sb("rope_sin", [P, TL, HD // 2], F32, s12)
        nsin = sb("rope_minus_sin", [P, TL, HD // 2], F32, s12)
        g_q = sb("b_q_gain", [P, HD], F32, s12)
        g_k = sb("b_k_gain", [P, HD], F32, s12)
        s1 = ExitStack()
        x5 = sb("x_tiles", [P, NT, D], F32, s1)
        stats = sb("x_stats", [P, NT, 12], F32, s1)
        mv = sb("x_mean_var", [P, NT, 2], F32, s1)
        var5 = sb("x_var", [P, NT], F32, s1)
        rstd5 = sb("x_rstd", [P, NT], F32, s1)
        half5 = sb("x_half", [P, NT], F32, s1)
        shift5 = sb("x_shift", [P, NT], I32, s1)
        h_mod = sb("h_modulated", [P, 2, NT * P], F32, s1)
        s1.close()
        s2 = ExitStack()
        rt = sb("rope_a", [P, CW], F32, s2)
        ru = sb("rope_b", [P, CW], F32, s2)
        rr = sb("rotated", [P, CW], F32, s2)
        sq = sb("squares", [P, CW], F32, s2)
        qn = sb("normed", [P, CW], F32, s2)
        ms8 = sb("mean_squares", [P, 8], F32, s2)
        rs8 = sb("rms_recip", [P, 8], F32, s2)
        hf8 = sb("rms_half", [P, 8], F32, s2)
        sh8 = sb("rms_shift", [P, 8], I32, s2)
        hl = sb("hi_lo", [P, 2, 8, 2, HD], F32R, s2)
        tst = sb("turned_staging", [P, TST, 8, P], F32, s2)
        vst = sb("value_staging", [P, 2, CW], F32, s2)
        pst = sb("prompt_k_staging", [P, 2, CW], F32, s2)
        mst = sb("mod_staging", [2, 2, CW], F32, s2)
        s2.close()
        s12.close()

        s3 = ExitStack()
        qtb.append(sb("q_bundle1", [P, REP, NT * P], F32R, s3))
        ktb.append(sb("k_bundle1", [P, 2, 2, KCOL], F32R, s3))
        vb.append(sb("v_bundle1", [P, NT + 1, P], F32, s3))
        PR, RR = 4, 8
        pbuf = sb("p_unnormed", [P, PR, NKEY], F32, s3)
        abuf = sb("p_difference", [P, 2, NKEY], F32, s3)
        ptb = sb("p_turned", [P, 2, NT, P], F32, s3)
        ost = sb("o_staging", [P, 2, NT, 2 * P], F32, s3)
        nmax = sb("minus_max", [P, RR], F32, s3)
        rsum = sb("p_sums", [P, RR], F32, s3)
        rinv = sb("p_sums_recip", [P, RR], F32, s3)
        coef = sb("map_coef", [P, 1], F32, s3)
        lam_in = sb("lambda_vectors", [P, 4, HD], F32, s3)
        lam_s = sb("lambda_sums", [P, 2], F32, s3)
        lam_e = sb("lambda_exps", [P, 2], F32, s3)
        nlam = sb("minus_lambda", [P, 1], F32, s3)
        s3.close()
        s3a.close()

        jobs, maps = [], []
        for bi, (kind, _) in enumerate(bundles):
            for r in range(REP if kind else 1):
                for tt in range(NT):
                    j = len(jobs)
                    jobs.append((bi, kind, r, tt, len(maps)))
                    maps += [(j, 0)] if kind else [(j, 0), (j, 1)]
        NJ, NM = len(jobs), len(maps)
        job_end = {bi: max(j for j, q in enumerate(jobs) if q[0] == bi) + 1 for bi in range(len(bundles))}
        bundle_in = [sem(f"bundle_in{i}") for i in range(2)]
        lam_in_s = sem("lambda_in")
        lam_sem = sem("lambda_steps")
        s_ready = sem("scores_ready")
        nb_done = sem("max_done")
        e_done = sem("exp_done")
        a_done = sem("difference_done")
        t_ready = sem("p_turned_ready")
        pt_full = [sem(f"p_turned_copied{i}") for i in range(2)]
        pv_ready = sem("pv_ready")
        o_out = sem("o_scaled")
        o_st = [sem(f"o_stored{i}") for i in range(2)]

        def spair(m):
            return pair[m % 2]

        def obank(j):
            return pair[3][:, (j % 2) * CW:(j % 2) * CW + P]

        def width(j):
            return P if jobs[j][3] == PROMPT else NKEY

        def copied_by_dve(j):
            return jobs[j][1] == 1 and j % 3 == 0

        def copy_turned(eng, copy, j):
            eng.wait_ge(t_ready, j + 1)
            if j >= 2:
                eng.wait_ge(pv_ready, j - 1)
            w = width(j)
            dst = ptb[:, j % 2].rearrange("p k q -> p (k q)")[:, 0:w]
            copy(dst, pair[2][:, 0:w]).then_inc(pt_full[j % 2], 1)
        s4 = ExitStack()
        ot_hi = [sb("oA_turned_hi", [P, KD, NT * P], F32R, s4)]
        ot_lo = [sb("oA_turned_lo", [P, KD, NT * P], F32R, s4)]
        rows = sb("rows", [P, NT, D], F32, s4)
        logit = sb("logits", [P, NT, NG + NE], F32, s4)
        slot_i = sb("slot_of_pair", [P, NT, 2], U32, s4)
        pair_w = sb("weight_of_pair", [P, NT, 2], F32, s4)
        ctl = sb("control", [P, 1 + TILES], I32, s4)
        zero = sb("zeros", [P, D], F32, s4)
        st4 = sb("row_stats", [P, 12], F32, s4)
        mv4 = sb("row_mean_var", [P, 2], F32, s4)
        va4 = sb("row_var", [P, 1], F32, s4)
        rs4 = sb("row_rstd", [P, 1], F32, s4)
        hf4 = sb("row_half", [P, 1], F32, s4)
        sh4 = sb("row_shift", [P, 1], I32, s4)
        before = sb("earlier_tokens", [P, P], F32, s4)
        ones = sb("ones", [P, P], F32, s4)
        tab = sb("tables", [P, TAB_W], F32, s4)
        s4a = ExitStack()
        ot_hi.append(sb("oB_turned_hi", [P, KD, NT * P], F32R, s4a))
        ot_lo.append(sb("oB_turned_lo", [P, KD, NT * P], F32R, s4a))
        oin = sb("o_rows", [P, 2, D], F32, s4a)
        gin = sb("gate_rows", [P, 2, CW], F32, s4a)
        sqb = sb("o_squares", [P, D], F32, s4a)
        gated = sb("gated_b", [P, CW], F32, s4a)
        oms = sb("o_mean_squares", [P, 8], F32, s4a)
        ors = sb("o_rms_recip", [P, 8], F32, s4a)
        ohf = sb("o_half", [P, 8], F32, s4a)
        osh = sb("o_shift", [P, 8], I32, s4a)
        gcol = sb("subln_gain", [P, 1], F32, s4a)
        s4a.close()
        s4b = ExitStack()
        yb = sb("y_rows", [P, 2, D], F32, s4b)
        xr = sb("x_rows", [P, 2, D], F32, s4b)
        ln1 = sb("ln1_gain_bias", [P, 2, D], F32, s4b)
        bc = sb("mod_rows", [P, 2, 3, D], F32, s4b)
        h2t = sb("h2_turned", [P, KD, P], F32, s4b)
        w_rt = sb("router_weights", [P, KD, NG + NE], F32, s4b)
        b_rt = sb("router_bias", [P, NG + NE], F32, s4b)
        s4b.close()
        s5 = ExitStack()
        mc = sb("coarse_max", [P, NT], F32, s5)
        oh_g = sb("group_pick", [P, NT, NG], F32, s5)
        ex = sb("exp_args", [P, NT, NG + 1], F32, s5)
        ee = sb("exps", [P, NT, NG + 1], F32, s5)
        prod = sb("route_products", [P, NT, NG, EPG], F32, s5)
        fs = sb("fine_logits", [P, NT, EPG], F32, s5)
        m1 = sb("fine_max", [P, NT], F32, s5)
        m2 = sb("fine_second", [P, NT], F32, s5)
        pk = [sb(f"fine_pick{i}", [P, NT, EPG], F32, s5) for i in range(2)]
        pri = sb("pick_priority", [P, NT], F32, s5)
        choice = [sb(f"expert_pick{i}", [P, NT, NG, EPG], F32, s5) for i in range(2)]
        mask = sb("expert_mask", [P, NT, NE], F32, s5)
        den = sb("weight_denom", [P, NT], F32, s5)
        posn = sb("positions", [P, NT + 1, NE], F32, s5)
        nov = sb("over_tiles", [P, NE], F32, s5)
        tri = sb("over_products", [P, NE, NE], F32, s5)
        ovc = sb("over_cumulated", [P, NE], F32, s5)
        v2 = sb("over_base", [P, NE], F32, s5)
        slotf = sb("slot_numbers", [P, NT, 2], F32, s5)
        cf = sb("control_f", [P, 1 + TILES], F32, s5)
        cle = sb("over_compare", [P, MORE, NE], F32, s5)
        s6 = ExitStack()
        xs = sb("expert_in", [P, 2, D], F32, s6)
        xt_hi = sb("expert_in_hi", [P, 2, KD, P], F32R, s6)
        xt_lo = sb("expert_in_lo", [P, 2, KD, P], F32R, s6)
        th = sb("gate_tanh_rows", [P, FF], F32, s6)
        ac = sb("expert_hidden", [P, FF], F32, s6)
        at_hi = sb("hidden_hi", [P, KF, P], F32R, s6)
        at_lo = sb("hidden_lo", [P, KF, P], F32R, s6)
        yo = sb("expert_out_rows", [P, 2, D], F32, s6)
        s6.close()
        s7 = ExitStack()
        ya = sb("first_expert_rows", [P, 2, D], F32, s7)
        yc = sb("second_expert_rows", [P, 2, D], F32, s7)
        xq = sb("x1_rows", [P, 2, D], F32, s7)
        g2 = sb("gate2_rows", [P, 2, D], F32, s7)
        ln2 = sb("ln2_gain_bias", [P, 2, D], F32, s7)
        s7.close()
        s5.close()

        exp_in = sem("route_exp_in")
        exp_out = sem("route_exp_out")
        ones_done = sem("ones_done")
        mask_done = sem("mask_done")
        pre_done = sem("positions_done")
        route_done = sem("route_done")
        scat_st = sem("rows_scattered")
        xs_in = [sem(f"expert_in{i}") for i in range(2)]
        x_turned = sem("expert_in_turned")
        xh_done = sem("expert_in_hi_done")
        xl_done = sem("expert_in_split")
        moe_blk = sem("moe_blocks")
        th_done = sem("gate_tanh_done")
        silu_done = sem("silu_done")
        hid_done = sem("hidden_done")
        aturned = sem("hidden_turned")
        ah_done = sem("hidden_hi_done")
        al_done = sem("hidden_split")
        y_copied = sem("expert_out_copied")
        y_st = [sem(f"expert_out_stored{i}") for i in range(2)]
        y_free = sem("expert_out_free")
        s7_in = sem("gate2_in")
        y_in = [sem(f"pair_rows_in{i}") for i in range(2)]
        x7_in = [sem(f"x1_rows_in{i}") for i in range(2)]
        f_done = sem("out_normed")
        fg_done = sem("out_scaled")
        fb_done = sem("out_done")
        out_st = [sem(f"out_stored{i}") for i in range(2)]
        w_gu = t["w_gate_up"][0].rearrange("e (k p) n -> p e k n", p=P)
        w_dn = t["w_down"][0].rearrange("e (k p) n -> p e k n", p=P)

        def expert_chunk(e, r, c):
            if r < 2:
                return w_gu[:, e, 2 * c:2 * c + 2, r * FF:(r + 1) * FF]
            return w_dn[:, e, 2 * (c % 2):2 * (c % 2) + 2, (c // 2) * CW:(c // 2 + 1) * CW]

        def last_pair_of_tiles(eng):
            return eng.value_load(ctl[0:1, 0:1], min_val=NE // 2 - 1, max_val=TILES // 2 - 1)
        s4.close()

        B_WA = NB - 6
        o_in = [sem(f"o_rows_in{i}") for i in range(2)]
        g_in = [sem(f"gate_rows_in{i}") for i in range(2)]
        gcol_in = sem("subln_gain_in")
        gcol_done = sem("subln_gain_done")
        osq_done = sem("o_squares_done")
        on_done = sem("o_normed")
        oh_done = sem("o_hi_done")
        ot_done = sem("o_split")
        mg_done = sem("merge_steps")
        mh_done = sem("merged_hi_done")
        mt_done = sem("merged_split")
        s4b_in = sem("ln1_in")
        bc_done = sem("mod_rows_done")
        x4_in = [sem(f"x_rows_in{i}") for i in range(2)]
        ya_done = sem("y_normed")
        x1_part = sem("x1_scaled")
        x1_done = sem("x1_done")
        x1_st = [sem(f"x1_stored{i}") for i in range(2)]
        yb_done = sem("h2_normed")
        h2_part = sem("h2_scaled")
        h2_done = sem("h2_done")
        h2t_done = sem("h2_turned_done")
        zero_done = sem("zeros_set")
        zero_st = sem("expert_rows_cleared")

        tail_no, n = {}, N_PJ + 4 * NT
        for tt in range(NT + 2):
            if tt < NT:
                tail_no["wo", tt, 0], tail_no["wo", tt, 1] = n, n + 1
                n += 2
            if tt >= 2:
                tail_no["L", tt - 2] = n
                n += 1
        for b in range(4):
            last_no[B_WA + b] = N_PJ + NT * (b + 1) - 1
        last_no[NB - 2], last_no[NB - 1] = tail_no["wo", NT - 1, 0], tail_no["wo", NT - 1, 1]
        TR_O, TR_M, TR_H = N_TR, N_TR + 2 * NT, N_TR + 3 * NT
        N_PJ2, N_TR2 = n, N_TR + 4 * NT

        def branch_block(v):
            return B_WA + v // NT
        block = ctx.enter_context(nc.Block())

        @block.sync
        def _(sp):
            for o, i in ((cond[:], t["conds"]), (ident[:], t["k_ident"]), (pick_cols[:], t["k_pick"])):
                sp.dma_start(o, i).then_inc(const_in, 16)
            for tt in range(NT):
                src = t["x_prompt"][0] if tt == PROMPT else t["x_sample"][0, tt * P:(tt + 1) * P]
                sp.dma_start(x5[:, tt], src).then_inc(x_in, 16)

            def weights(b):
                for c in range(NC_CH):
                    if b:
                        sp.wait_ge(lo_done, NC_CH * (b - 1) + c + 1)
                    sp.dma_start(w_raw[:, c], block_chunk(b, c)).then_inc(raw_in[c], 16)

            for b in range(4):
                weights(b)
            sp.dma_start(cosd[:], t["k_cos"].rearrange("(t p) d -> p t d", p=P)).then_inc(cache_in, 16)
            sp.dma_start(sind[:], t["k_sin"].rearrange("(t p) d -> p t d", p=P)).then_inc(cache_in, 16)
            sp.dma_start(nsin[:], t["k_nsin"].rearrange("(t p) d -> p t d", p=P)).then_inc(cache_in, 16)
            sp.dma_start(g_q[:], t["b_q_g"][0:1, :].to_broadcast([P, HD])).then_inc(cache_in, 16)
            sp.dma_start(g_k[:], t["b_k_g"][0:1, :].to_broadcast([P, HD])).then_inc(cache_in, 16)
            sp.dma_start(cache[:, 0:D], t["cache_a_k"][0, 0].rearrange("s h n d -> s (h n d)")).then_inc(cache_in, 16)
            sp.dma_start(cache[:, D:], t["cache_b_k"][0, 0].rearrange("s h d -> s (h d)")).then_inc(cache_in, 16)
            for b in range(4, NB):
                weights(b)
            def tile_weights(tile, chunk):
                for r in range(3):
                    for c in range(NC_CH):
                        sp.wait_ge(lo_done, NC_CH * (NB + 3 * tile + r - 1) + c + 1)
                        sp.dma_start(w_raw[:, c], chunk(r, c)).then_inc(raw_in[c], 16)

            for s in range(2):
                tile_weights(s, lambda r, c: expert_chunk(s, r, c))
            sp.wait_ge(route_done, 1)
            last_pair = last_pair_of_tiles(sp)
            with sp.Fori(1, last_pair + 1) as i:
                for s in range(2):
                    e = sp.value_load(ctl[0:1, bass.ds(1 + 2 * i + s, 1)], min_val=0, max_val=NE - 1)
                    tile_weights(2 * i + s, lambda r, c: expert_chunk(bass.ds(e, 1), r, c).rearrange(
                        "p o k n -> p (o k) n"))

        @block.scalar
        def _(act):
            def split_hi(b):
                for c in range(NC_CH):
                    act.wait_ge(raw_in[c], 16 * (b + 1))
                    if b >= 2:
                        act.wait_ge(pj_ready, last_no[b - 2] + 1)
                    act.copy(w_hi[:, b % 2, c], w_raw[:, c]).then_inc(hi_done, 1)

            def after(i):
                kind = units[i][0]
                for j, n in zip(tst_no.get(i, []), tr_no[i]):
                    act.wait_ge(tr_ready, n + 1)
                    if j >= TST:
                        act.wait_ge(tst_st[j % TST], tst_sum[j - TST])
                    nm = B_KV if kind in ("bkv", "cbk") else 8
                    act.activation(tst[:, j % TST, 0:nm].rearrange("p m q -> p (m q)"), turned(n)[:, 0:nm * P],
                                   ACT.Copy, scale=SCALE if kind in ("q", "bq") else 1.0).then_inc(tr_free[n % 2], 1)

            def post(i):
                kind, b, ci, tt = units[i]
                if kind == "ada":
                    act.wait_ge(pj_ready, pj_no[i] + 1)
                    if ci >= 2:
                        prev = [q for q, u in enumerate(units) if u[0] == "ada" and u[2] == ci - 2][0]
                        act.wait_ge(tr_ready, tr_no[prev][0] + 1)
                    act.copy(stage5[0:4, ci % 2], bank(pj_no[i])[0:4]).then_inc(pj_free[pj_no[i] % 4], 1)
                elif kind in ("v", "g", "bkv"):
                    n, j = pj_no[i], vst_no[i]
                    act.wait_ge(pj_ready, n + 1)
                    if j >= 2:
                        act.wait_ge(vst_st[j % 2], vst_sum[j - 2])
                    if kind == "g":
                        act.activation(vst[:, j % 2], bank(n), ACT.Tanh, scale=0.5).then_inc(pj_free[n % 4], 1)
                    elif kind == "v":
                        act.copy(vst[:, j % 2], bank(n)).then_inc(pj_free[n % 4], 1)
                    else:
                        act.copy(vst[:, j % 2, 0:256], bank(n)[:, 256:512]).then_inc(v_out, 1)
                if kind in ("bq", "bkv"):
                    n = pj_no[i]
                    w = 512 if kind == "bq" else 256
                    act.wait_ge(pj_ready, n + 1)
                    k = sum(u[0] in ("bq", "bkv") for u in units[:i])
                    if k:
                        act.wait_ge(hl_done, hl_no[[q for q in range(i) if units[q][0] in ("bq", "bkv")][-1]] + 1)
                    act.activation(sq[:, 0:w], bank(n)[:, 0:w], ACT.Square).then_inc(sq_done, 1)

            act.wait_ge(const_in, 48)
            act.activation(cond_t[:], cond[:], ACT.Tanh, scale=0.5).then_inc(cond_silu, 1)
            split_hi(0)
            for i in range(N_EARLY):
                split_hi(i + 1)
                post(i)
            for k in range(KD):
                n = H_GROUP0 + k
                act.wait_ge(tr_ready, n + 1)
                if k == 0:
                    act.wait_ge(tr_free[1], 2)
                    act.wait_ge(tr_free[0], 2)
                if k >= 2:
                    act.wait_ge(h_done, k - 1)
                act.activation(h_mod[:, k % 2, 0:N_LAT], turned(n)[:, 0:N_LAT], ACT.Identity,
                               bias=mod_t[:, k, 1:2], scale=mod_t[:, KD + k, 1:2])
                act.activation(h_mod[:, k % 2, N_LAT:], turned(n)[:, N_LAT:NT * P], ACT.Identity,
                               bias=mod_t[:, k, 0:1], scale=mod_t[:, KD + k, 0:1]).then_inc(tr_free[n % 2], 1)
            for i in range(N_EARLY, len(units)):
                if first_of_block(i):
                    split_hi(units[i][1] + 1)
                post(i)
                if i - 2 >= N_EARLY:
                    after(i - 2)
            after(len(units) - 2)
            after(len(units) - 1)
            act.wait_ge(lam_sem, 1)
            act.activation(lam_e[:], lam_s[:], ACT.Exp).then_inc(lam_sem, 1)
            for j in range(NJ + 2):
                if j < NJ:
                    for m in [m for m in range(jobs[j][4], NM) if maps[m][0] == j]:
                        act.wait_ge(nb_done, m + 1)
                        if m >= PR:
                            jl = maps[m - PR][0]
                            act.wait_ge(*((t_ready, jl + 1) if jobs[jl][1] else (a_done, jl + 1)))
                        if m >= RR:
                            act.wait_ge(o_out, maps[m - RR][0] + 1)
                        w = width(j)
                        act.activation(pbuf[:, m % PR, 0:w], spair(m)[:, 0:w], ACT.Exp, bias=nmax[:, m % RR:m % RR + 1],
                                       accum_out=rsum[:, m % RR:m % RR + 1]).then_inc(e_done, 1)
                if 2 <= j and not copied_by_dve(j - 2):
                    copy_turned(act, act.copy, j - 2)
            act.wait_ge(o_out, NJ)
            for i in range(2):
                act.wait_ge(o_st[i], 16 * (len(bundles) // 2))

            def square(z):
                if z < NT:
                    act.wait_ge(o_in[z % 2], 16 * (z // 2 + 1))
                    if z:
                        act.wait_ge(on_done, z)
                    act.activation(sqb[:], oin[:, z % 2], ACT.Square).then_inc(osq_done, 1)

            def round_o(z):
                n = TR_O + z
                cols = slice((z % NT) * P, (z % NT + 1) * P)
                act.wait_ge(tr_ready, n + 1)
                if z == 0:
                    act.wait_ge(gcol_done, 1)
                src = turned(n)[:].rearrange("p (k q) -> p k q", q=P)
                act.activation(ot_hi[z // NT][:, :, cols], src, ACT.Copy,
                               scale=gcol[:] if z < NT else 1.0).then_inc(oh_done, 1)

            def round_merged(tt):
                n = TR_M + tt
                act.wait_ge(tr_ready, n + 1)
                act.activation(ot_hi[0][:, :, tt * P:(tt + 1) * P], turned(n)[:].rearrange("p (k q) -> p k q", q=P),
                               ACT.Copy, scale=0.5).then_inc(mh_done, 1)

            square(0)
            square(1)
            for v in range(4 * NT):
                if v % NT == 0:
                    split_hi(branch_block(v) + 1)
                if v < 2 * NT:
                    round_o(v)
                    square(v + 2)
                if v >= 3 * NT + 2:
                    round_merged(v - 3 * NT - 2)
            round_merged(NT - 2)
            round_merged(NT - 1)
            split_hi(NB - 1)
            for tt in range(NT):
                n = TR_H + tt
                act.wait_ge(tr_ready, n + 1)
                if tt:
                    act.wait_ge(pj_ready, tail_no["L", tt - 1] + 1)
                act.copy(h2t[:].rearrange("p k q -> p (k q)"), turned(n)[:]).then_inc(tr_free[n % 2], 1)
            act.wait_ge(exp_in, 1)
            act.activation(ee[:], ex[:], ACT.Exp).then_inc(exp_out, 1)
            for sm in (xh_done, th_done, ah_done, y_copied):
                act.nop().then_inc(sm, OFF)
            act.wait_ge(pj_ready, N_PJ2)

            def split_hi_moe(q):
                par, tile3 = q
                for c in range(NC_CH):
                    act.wait_ge(raw_in[c], 16 * (NB + tile3 + 1))
                    act.wait_ge(moe_blk, tile3 - 1 + OFF)
                    act.copy(w_hi[:, par, c], w_raw[:, c]).then_inc(hi_done, 1)

            def round_x(tile, s):
                act.wait_ge(x_turned, tile + 1 + OFF)
                act.copy(xt_hi[:, s].rearrange("p k q -> p (k q)"), pair[1][:]).then_inc(xh_done, 1)

            def act_tile(i, s, final):
                tile, q = 2 * i + s, 6 * i + 3 * s
                par = (NB + 3 * s) % 2
                split_hi_moe(((par + 1) % 2, q + 1))
                act.wait_ge(moe_blk, q + 1 + OFF)
                act.wait_ge(hid_done, tile + OFF)
                act.activation(th[:], pair[0][:, 0:FF], ACT.Tanh, scale=0.5).then_inc(th_done, 1)
                split_hi_moe((par, q + 2))
                if not final:
                    round_x(tile + 1, 1 - s)
                act.wait_ge(aturned, tile + 1 + OFF)
                act.activation(at_hi[:].rearrange("p k q -> p (k q)"), pair[2][:, 0:FF], ACT.Copy,
                               scale=0.5).then_inc(ah_done, 1)
                if not final:
                    split_hi_moe(((par + 1) % 2, q + 3))
                act.wait_ge(moe_blk, q + 3 + OFF)
                act.wait_ge(y_free, tile - 1 + OFF)
                act.copy(yo[:, s], pair[3][:]).then_inc(y_copied, 1)

            act.wait_ge(route_done, 1)
            last_pair = last_pair_of_tiles(act)
            act.wait_ge(y_free, OFF)
            split_hi_moe((NB % 2, 0))
            round_x(0, 0)
            with act.Fori(0, last_pair) as i:
                for s in range(2):
                    act_tile(i, s, False)
            act_tile(last_pair, 0, False)
            act_tile(last_pair, 1, True)

        @block.vector
        def _(dve):
            link = chain(dve, dve_link)

            def split_lo(b):
                for c in range(NC_CH):
                    dve.wait_ge(hi_done, NC_CH * b + c + 1)
                    dve.tensor_tensor(w_lo[:, b % 2, c], w_raw[:, c], w_hi[:, b % 2, c].bitcast(F32),
                                      ALU.subtract).then_inc(lo_done, 1)

            def split_heads(i, src, nh):
                j = hl_no[i]
                if j >= 2:
                    dve.wait_ge(tr_ready, tr_no[hl_users[j - 2]][-1] + 1)
                s = src.rearrange("p (m d) -> p m d", d=HD)
                hi, lo = hl[:, j % 2, 0:nh, 0], hl[:, j % 2, 0:nh, 1]
                link(dve.tensor_copy(hi, s))
                dve.tensor_tensor(lo, s, hi.bitcast(F32), ALU.subtract).then_inc(hl_done, 1)
                dve.wait_ge(hl_done, hl_no[i] + 1)

            def rope(x, nh, tt, free):
                w = nh * HD
                xv = x.rearrange("p (m e two) -> p m e two", m=nh, two=2)
                uv = ru[:, 0:w].rearrange("p (m e two) -> p m e two", m=nh, two=2)
                xs = x.rearrange("p (m d) -> p m d", m=nh)
                dve.tensor_tensor(rt[:, 0:w].rearrange("p (m d) -> p m d", m=nh), xs,
                                  over(cosd[:, tt], 1, [P, nh, HD]), ALU.mult)
                dve.tensor_tensor(uv[:, :, :, 0], xv[:, :, :, 1], over(nsin[:, tt], 1, [P, nh, HD // 2]), ALU.mult)
                last = dve.tensor_tensor(uv[:, :, :, 1], xv[:, :, :, 0], over(sind[:, tt], 1, [P, nh, HD // 2]),
                                         ALU.mult)
                if free is None:
                    link(last)
                else:
                    sm, val = free
                    last.then_inc(sm, 1)
                    dve.wait_ge(sm, val)
                link(dve.tensor_tensor(rr[:, 0:w], rt[:, 0:w], ru[:, 0:w], ALU.add))

            def post(i):
                kind, b, ci, tt = units[i]
                if kind == "ck":
                    if ci == 0:
                        dve.wait_ge(cache_in, 112)
                    split_heads(i, cache[:, ci * CW:(ci + 1) * CW], 8)
                elif kind == "cbk":
                    split_heads(i, cache[:, D:], B_KV)
                elif kind in ("q", "k"):
                    n = pj_no[i]
                    dve.wait_ge(pj_ready, n + 1)
                    free = (pj_free[n % 4], n // 4 + 1)
                    if n == 4:
                        dve.wait_ge(cache_in, 112)
                    if tt != PROMPT:
                        rope(bank(n), 8, tt, free)
                        split_heads(i, rr[:], 8)
                    elif kind == "q":
                        dve.tensor_copy(rr[:], bank(n)).then_inc(free[0], 1)
                        dve.wait_ge(*free)
                        split_heads(i, rr[:], 8)
                    else:
                        s = pst_no[i]
                        if s >= 2:
                            dve.wait_ge(pst_st[s % 2], 16 * (s // 2))
                        dve.tensor_copy(pst[:, s % 2], bank(n)).then_inc(free[0], 1)
                        dve.wait_ge(*free)
                        split_heads(i, pst[:, s % 2], 8)
                elif kind in ("bq", "bkv"):
                    n = pj_no[i]
                    w, nh = (512, 8) if kind == "bq" else (256, 4)
                    gain = g_q if kind == "bq" else g_k
                    k = sum(u[0] in ("bq", "bkv") for u in units[:i])
                    dve.wait_ge(sq_done, k + 1)
                    s3 = "p (m d) -> p m d"
                    link(dve.tensor_reduce(ms8[:, 0:nh], sq[:, 0:w].rearrange(s3, d=HD), AX.X, ALU.add))
                    link(dve.tensor_scalar(ms8[:, 0:nh], ms8[:, 0:nh], 1.0 / HD, EPS, ALU.mult, ALU.add))
                    rsqrt(dve, link, rs8[:, 0:nh], ms8[:, 0:nh], hf8[:, 0:nh], sh8[:, 0:nh])
                    if kind == "bkv":
                        dve.wait_ge(v_out, sum(u[0] == "bkv" for u in units[:i + 1]))
                    dve.tensor_tensor(qn[:, 0:w].rearrange(s3, d=HD), bank(n)[:, 0:w].rearrange(s3, d=HD),
                                      over(rs8[:, 0:nh], 2, [P, nh, HD]), ALU.mult).then_inc(pj_free[n % 4], 1)
                    dve.wait_ge(pj_free[n % 4], n // 4 + 1)
                    if kind == "bkv" and tt == PROMPT:
                        s = pst_no[i]
                        dve.wait_ge(pst_st[s % 2], 16 * (s // 2))
                        dst = pst[:, s % 2, 0:w]
                    else:
                        dst = qn[:, 0:w]
                    link(dve.tensor_tensor(dst.rearrange(s3, d=HD), qn[:, 0:w].rearrange(s3, d=HD),
                                           over(gain[:], 1, [P, nh, HD]), ALU.mult))
                    if tt != PROMPT:
                        rope(qn[:, 0:w], nh, tt, None)
                        split_heads(i, rr[:, 0:w], nh)
                    else:
                        split_heads(i, dst, nh)

            def after(i):
                kind, b, ci, tt = units[i]
                if kind != "ada":
                    return
                n = tr_no[i][0]
                dve.wait_ge(tr_ready, n + 1)
                if ci < 4:
                    dst = mod_t[:, 4 * ci:4 * ci + 4].rearrange("p k c -> p (k c)")
                    if ci < 2:
                        dve.tensor_copy(dst, turned(n)[:, 0:8]).then_inc(tr_free[n % 2], 1)
                    else:
                        dve.tensor_scalar(dst, turned(n)[:, 0:8], 1.0, None, ALU.add).then_inc(tr_free[n % 2], 1)
                else:
                    m = ms_no[i]
                    if m >= 2:
                        dve.wait_ge(ms_st[m % 2], 16 * (m // 2))
                    dve.tensor_copy(mst[:, m % 2], turned(n)[0:2, 0:CW]).then_inc(tr_free[n % 2], 1)

            dve.wait_ge(cond_silu, 1)
            link(dve.scalar_tensor_tensor(cond_t[:], cond_t[:], 1.0, cond[:], ALU.add, ALU.mult))
            link(dve.tensor_scalar(cond_t[:], cond_t[:], 0.5, None, ALU.mult))
            link(dve.tensor_copy(cond_hl[:, :, 0:2], cond_t[:]))
            dve.tensor_tensor(cond_hl[:, :, 2:4], cond_t[:], cond_hl[:, :, 0:2].bitcast(F32),
                              ALU.subtract).then_inc(cond_silu, 1)
            split_lo(0)
            for tt in range(NT):
                dve.wait_ge(x_in, 16 * NT)
                for h in range(2):
                    last = dve.bn_stats(stats[:, tt, 6 * h:6 * h + 6], x5[:, tt, h * CW:(h + 1) * CW])
                link(last)
                link(dve.bn_aggr(mv[:, tt], stats[:, tt]))
            link(dve.tensor_scalar(var5[:], mv[:, :, 1], EPS, None, ALU.add))
            rsqrt(dve, link, rstd5[:], var5[:], half5[:], shift5[:])
            for tt in range(NT):
                dve.tensor_scalar(x5[:, tt], x5[:, tt], mv[:, tt, 0:1], rstd5[:, tt:tt + 1],
                                  ALU.subtract, ALU.mult).then_inc(norm_done, 1)
            for i in range(N_EARLY):
                split_lo(i + 1)
                if i:
                    after(i - 1)
            after(N_EARLY - 1)
            for k in range(KD):
                dve.wait_ge(tr_free[(H_GROUP0 + k) % 2], (H_GROUP0 + k) // 2 + 1)
                link(dve.tensor_copy(h_hi[:, k], h_mod[:, k % 2]))
                dve.tensor_tensor(h_lo[:, k], h_mod[:, k % 2], h_hi[:, k].bitcast(F32),
                                  ALU.subtract).then_inc(h_done, 1)
            for i in range(N_EARLY, len(units)):
                if first_of_block(i):
                    split_lo(units[i][1] + 1)
                post(i)
                if i - 2 >= N_EARLY:
                    after(i - 2)
            after(len(units) - 2)
            after(len(units) - 1)
            dve.wait_ge(lam_in_s, 64)
            link(dve.tensor_tensor(lam_in[:, 0:4:2], lam_in[:, 0:4:2], lam_in[:, 1:4:2], ALU.mult))
            dve.tensor_reduce(lam_s[:], lam_in[:, 0:4:2], AX.X, ALU.add).then_inc(lam_sem, 1)
            dve.wait_ge(lam_sem, 2)
            link(dve.tensor_tensor(nlam[:], lam_e[:, 1:2], lam_e[:, 0:1], ALU.subtract))
            link(dve.tensor_scalar(nlam[:], nlam[:], -LAMBDA_INIT, None, ALU.add))
            for j in range(NJ + 4):
                if j < NJ:
                    for m in [m for m in range(jobs[j][4], NM) if maps[m][0] == j]:
                        dve.wait_ge(s_ready, m + 1)
                        if m >= RR:
                            dve.wait_ge(e_done, m - RR + 1)
                        dve.tensor_reduce(nmax[:, m % RR:m % RR + 1], spair(m)[:, 0:width(j)], AX.X, ALU.max,
                                          negate=True).then_inc(nb_done, 1)
                i = j - 1
                if 0 <= i < NJ and jobs[i][1] == 0:
                    m, w = jobs[i][4], width(i)
                    s0, s1_ = m % RR, m % RR + 1
                    dve.wait_ge(e_done, m + 2)
                    if i >= 2:
                        dve.wait_ge(t_ready, i - 1)
                    link(dve.reciprocal(rinv[:, s0:s0 + 2], rsum[:, s0:s0 + 2]))
                    link(dve.scalar_tensor_tensor(coef[:], rsum[:, s0:s0 + 1], nlam[:], rinv[:, s1_:s1_ + 1], ALU.mult, ALU.mult))
                    dve.scalar_tensor_tensor(abuf[:, i % 2, 0:w], pbuf[:, (m + 1) % PR, 0:w], coef[:], pbuf[:, m % PR, 0:w],
                                             ALU.mult, ALU.add).then_inc(a_done, 1)
                    dve.wait_ge(a_done, i + 1)
                i = j - 2
                if 0 <= i < NJ and copied_by_dve(i):
                    copy_turned(dve, dve.tensor_copy, i)
                i = j - 4
                if 0 <= i < NJ:
                    bi, kind, r, tt, m = jobs[i]
                    slot, w = m % RR, HD if kind else P
                    if kind:
                        link(dve.reciprocal(rinv[:, slot:slot + 1], rsum[:, slot:slot + 1]))
                    dve.wait_ge(pv_ready, i + 1)
                    if bi >= 2:
                        dve.wait_ge(o_st[bi % 2], 16 * (bi // 2))
                    dve.tensor_scalar(ost[:, bi % 2, tt, r * HD:r * HD + w], obank(i)[:, 0:w], rinv[:, slot:slot + 1], None,
                                      ALU.mult).then_inc(o_out, 1)
            dve.wait_ge(pv_ready, NJ)
            for i in range(2):
                dve.wait_ge(o_st[i], 16 * (len(bundles) // 2))
            dve.memset(zero[:], 0.0).then_inc(zero_done, 1)
            dve.wait_ge(gcol_in, 16)
            dve.tensor_scalar(gcol[:], gcol[:], 1.0 - LAMBDA_INIT, None, ALU.mult).then_inc(gcol_done, 1)
            dve.wait_ge(gcol_done, 1)

            def norm_o(z):
                if z >= NT:
                    return
                dve.wait_ge(osq_done, z + 1)
                link(dve.tensor_reduce(oms[:], sqb[:].rearrange("p (h d) -> p h d", d=P), AX.X, ALU.add))
                link(dve.tensor_scalar(oms[:], oms[:], 1.0 / P, EPS, ALU.mult, ALU.add))
                rsqrt(dve, link, ors[:], oms[:], ohf[:], osh[:])
                o = oin[:, z % 2].rearrange("p (h d) -> p h d", d=P)
                dve.tensor_tensor(o, o, over(ors[:], 2, [P, A_HEADS, P]), ALU.mult).then_inc(on_done, 1)
                dve.wait_ge(on_done, z + 1)

            def rest_o(z):
                n = TR_O + z
                cols = slice((z % NT) * P, (z % NT + 1) * P)
                dve.wait_ge(oh_done, z + 1)
                dve.scalar_tensor_tensor(ot_lo[z // NT][:, :, cols], turned(n)[:].rearrange("p (k q) -> p k q", q=P),
                                         gcol[:] if z < NT else 1.0, ot_hi[z // NT][:, :, cols].bitcast(F32),
                                         ALU.mult, ALU.subtract).then_inc(tr_free[n % 2], 1)

            def rest_merged(tt):
                n = TR_M + tt
                cols = slice(tt * P, (tt + 1) * P)
                dve.wait_ge(mh_done, tt + 1)
                dve.scalar_tensor_tensor(ot_lo[0][:, :, cols], turned(n)[:].rearrange("p (k q) -> p k q", q=P),
                                         0.5, ot_hi[0][:, :, cols].bitcast(F32),
                                         ALU.mult, ALU.subtract).then_inc(tr_free[n % 2], 1)

            def merge(v):
                n, tt = N_PJ + v, v % NT
                part = rows[:, tt, (v // (2 * NT)) * CW:(v // (2 * NT) + 1) * CW]
                dve.wait_ge(pj_ready, n + 1)
                dve.wait_ge(g_in[v % 2], 16 * (v // 2 + 1))
                second = (v // NT) % 2
                dve.scalar_tensor_tensor(gated[:] if second else part, gin[:, v % 2], 1.0, bank(n),
                                         ALU.add, ALU.mult).then_inc(pj_free[n % 4], 1)
                dve.wait_ge(pj_free[n % 4], n // 4 + 1)
                if second:
                    dve.tensor_tensor(part, part, gated[:], ALU.add).then_inc(mg_done, 1)
                else:
                    dve.nop().then_inc(mg_done, 1)
                dve.wait_ge(mg_done, v + 1)

            norm_o(0)
            norm_o(1)
            for v in range(4 * NT):
                if v % NT == 0:
                    split_lo(branch_block(v) + 1)
                if v < 2 * NT:
                    rest_o(v)
                if v:
                    merge(v - 1)
                if v < 2 * NT:
                    norm_o(v + 2)
                if v >= 3 * NT + 2:
                    rest_merged(v - 3 * NT - 2)
            merge(4 * NT - 1)
            rest_merged(NT - 2)
            rest_merged(NT - 1)
            split_lo(NB - 1)

            def row_norm(src, dst, done):
                for h in range(2):
                    last = dve.bn_stats(st4[:, 6 * h:6 * h + 6], src[:, h * CW:(h + 1) * CW])
                link(last)
                link(dve.bn_aggr(mv4[:], st4[:]))
                link(dve.tensor_scalar(va4[:], mv4[:, 1:2], EPS, None, ALU.add))
                rsqrt(dve, link, rs4[:], va4[:], hf4[:], sh4[:])
                sm, val = done
                dve.tensor_scalar(dst, src, mv4[:, 0:1], rs4[:], ALU.subtract, ALU.mult).then_inc(sm, 1)
                dve.wait_ge(sm, val)

            def first_norm(tt):
                cnd = 0 if tt == PROMPT else 1
                y = yb[:, tt % 2]
                if tt >= 2:
                    dve.wait_ge(x1_st[tt % 2], 16 * (tt // 2))
                for h in range(2):
                    n = tail_no["wo", tt, h]
                    dve.wait_ge(pj_ready, n + 1)
                    c = slice(h * CW, (h + 1) * CW)
                    dve.tensor_tensor(y[:, c], bank(n), bc[:, cnd, 0, c], ALU.mult).then_inc(pj_free[n % 4], 1)
                dve.wait_ge(pj_free[n % 4], n // 4 + 1)
                dve.wait_ge(x4_in[tt % 2], 16 * (tt // 2 + 1))
                link(dve.scalar_tensor_tensor(y, xr[:, tt % 2], ALPHA, y, ALU.mult, ALU.add))
                row_norm(y, y, (ya_done, tt + 1))

            def second_norm(tt):
                dve.wait_ge(x1_done, tt + 1)
                row_norm(yb[:, tt % 2], rows[:, tt], (yb_done, tt + 1))

            def take_logits(tt):
                n = tail_no["L", tt]
                dve.wait_ge(pj_ready, n + 1)
                dve.tensor_tensor(logit[:, tt], bank(n)[:, 0:NG + NE], b_rt[:], ALU.add).then_inc(pj_free[n % 4], 1)
                dve.wait_ge(pj_free[n % 4], n // 4 + 1)

            dve.wait_ge(s4b_in, 14 * 16)
            dve.tensor_scalar(bc[:, :, 2], bc[:, :, 2], 1.0, None, ALU.add).then_inc(bc_done, 1)
            for tt in range(NT + 1):
                if tt < NT:
                    first_norm(tt)
                if tt:
                    second_norm(tt - 1)
                if tt >= 2:
                    take_logits(tt - 2)
            take_logits(NT - 1)
            dve.wait_ge(h2_done, NT)
            dve.wait_ge(x1_st[0], 16 * 3)
            dve.wait_ge(x1_st[1], 16 * 2)
            dve.memset(ones[:], 1.0).then_inc(ones_done, 1)
            lc, lf = logit[:, :, 0:NG], logit[:, :, NG:].rearrange("p t (g e) -> p t g e", g=NG)
            w4 = over(tab[:, T_PRI:T_PRI + NG], 1, [P, NT, NG])

            def pick_max(dst, src, top):
                link(dve.tensor_reduce(top, src, AX.X, ALU.max))
                link(dve.tensor_tensor(dst, src, over(top, 2, [P, NT, NG]), ALU.is_equal))
                link(dve.tensor_tensor(dst, dst, w4, ALU.mult))
                link(dve.tensor_reduce(pri[:], dst, AX.X, ALU.max))
                link(dve.tensor_tensor(dst, dst, over(pri[:], 2, [P, NT, NG]), ALU.is_equal))

            pick_max(oh_g[:], lc, mc[:])
            link(dve.tensor_tensor(ex[:, :, 0:NG], lc, over(mc[:], 2, [P, NT, NG]), ALU.subtract))
            link(dve.tensor_tensor(prod[:], lf, over(oh_g[:], 3, [P, NT, NG, EPG]), ALU.mult))
            link(dve.tensor_reduce(fs[:], prod[:].rearrange("p t g e -> p t e g"), AX.X, ALU.add))
            pick_max(pk[0][:], fs[:], m1[:])
            link(dve.scalar_tensor_tensor(fs[:], pk[0][:], -3.0e38, fs[:], ALU.mult, ALU.add))
            pick_max(pk[1][:], fs[:], m2[:])
            dve.tensor_tensor(ex[:, :, NG], m2[:], m1[:], ALU.subtract).then_inc(exp_in, 1)
            for i in range(2):
                link(dve.tensor_tensor(choice[i][:], over(oh_g[:], 3, [P, NT, NG, EPG]),
                                       over(pk[i][:], 2, [P, NT, NG, EPG]), ALU.mult))
            pick = [x[:].rearrange("p t g e -> p t (g e)") for x in choice]
            dve.tensor_tensor(mask[:], pick[0], pick[1], ALU.add).then_inc(mask_done, 1)
            dve.wait_ge(exp_out, 1)
            link(dve.tensor_reduce(den[:], ee[:, :, 0:NG], AX.X, ALU.add))
            link(dve.scalar_tensor_tensor(den[:], ee[:, :, NG], 1.0, den[:], ALU.add, ALU.mult))
            link(dve.reciprocal(pair_w[:, :, 0], den[:]))
            link(dve.tensor_tensor(pair_w[:, :, 1], pair_w[:, :, 0], ee[:, :, NG], ALU.mult))
            dve.wait_ge(pre_done, 1)
            link(dve.tensor_copy(posn[:].rearrange("p t e -> p (t e)"), pair[0][:, 0:(NT + 1) * NE]))
            cnt = posn[:, NT]
            link(dve.tensor_scalar(nov[:], cnt, float(P), None, ALU.is_gt))
            for k in range(2, NT):
                link(dve.scalar_tensor_tensor(nov[:], cnt, float(k * P), nov[:], ALU.is_gt, ALU.add))
            link(dve.tensor_tensor(tri[:], tab[:, T_TRI:T_ROW].rearrange("p (a b) -> p a b", a=NE),
                                   over(nov[:], 1, [P, NE, NE]), ALU.mult))
            link(dve.tensor_reduce(ovc[:], tri[:], AX.X, ALU.add))
            v1 = tab[:, T_ROW:T_ROW + NE]
            link(dve.tensor_tensor(v2[:], ovc[:], nov[:], ALU.subtract))
            link(dve.tensor_scalar(v2[:], v2[:], float(NE - 1), float(P), ALU.add, ALU.mult))
            link(dve.tensor_tensor(v2[:], v2[:], v1, ALU.subtract))
            pos = posn[:, 0:NT]
            p16 = prod[:].rearrange("p t g e -> p t (g e)")
            link(dve.scalar_tensor_tensor(p16, pos, float(P), over(v2[:], 1, [P, NT, NE]), ALU.is_ge, ALU.mult))
            link(dve.tensor_tensor(pos, pos, p16, ALU.add))
            link(dve.tensor_tensor(pos, pos, over(v1, 1, [P, NT, NE]), ALU.add))
            for i in range(2):
                link(dve.tensor_tensor(p16, pos, pick[i], ALU.mult))
                link(dve.tensor_reduce(slotf[:, :, i], p16, AX.X, ALU.add))
            link(dve.tensor_copy(slot_i[:], slotf[:]))
            link(dve.tensor_tensor(cle[:, 0, 0:MORE // 2], ovc[:, NE - 1:NE].to_broadcast([P, MORE // 2]),
                                   tab[:, T_PAIR:T_PAIR + MORE // 2], ALU.is_gt))
            link(dve.tensor_reduce(cf[:, 0:1], cle[:, 0, 0:MORE // 2], AX.X, ALU.add))
            link(dve.tensor_scalar(cf[:, 0:1], cf[:, 0:1], float(NE // 2 - 1), None, ALU.add))
            link(dve.tensor_copy(cf[:, 1:1 + TILES], tab[:, T_TILE:T_TILE + TILES]))
            link(dve.tensor_tensor(cle[:], over(ovc[:], 1, [P, MORE, NE]),
                                   over(tab[:, T_MORE:T_MORE + MORE], 2, [P, MORE, NE]), ALU.is_le))
            link(dve.tensor_reduce(cf[:, 1 + NE:], cle[:], AX.X, ALU.add))
            link(dve.tensor_scalar(cf[:, 1 + NE:], cf[:, 1 + NE:], float(NE - 1), None, ALU.min))
            dve.tensor_copy(ctl[:], cf[:]).then_inc(route_done, 1)
            for sm in (xl_done, silu_done, hid_done, al_done):
                dve.nop().then_inc(sm, OFF)

            def split_lo_moe(q):
                par, tile3 = q
                for c in range(NC_CH):
                    dve.wait_ge(hi_done, NC_CH * (NB + tile3) + c + 1)
                    dve.tensor_tensor(w_lo[:, par, c], w_raw[:, c], w_hi[:, par, c].bitcast(F32),
                                      ALU.subtract).then_inc(lo_done, 1)

            def rest_x(tile, s):
                dve.wait_ge(xh_done, tile + 1 + OFF)
                dve.tensor_tensor(xt_lo[:, s].rearrange("p k q -> p (k q)"), pair[1][:],
                                  xt_hi[:, s].rearrange("p k q -> p (k q)").bitcast(F32), ALU.subtract).then_inc(xl_done, 1)

            def dve_tile(i, s, final):
                tile, q = 2 * i + s, 6 * i + 3 * s
                par = (NB + 3 * s) % 2
                split_lo_moe(((par + 1) % 2, q + 1))
                dve.wait_ge(th_done, tile + 1 + OFF)
                dve.wait_ge(aturned, tile + OFF)
                dve.scalar_tensor_tensor(ac[:], th[:], 1.0, pair[0][:, 0:FF], ALU.add, ALU.mult).then_inc(silu_done, 1)
                split_lo_moe((par, q + 2))
                dve.wait_ge(moe_blk, q + 2 + OFF)
                dve.wait_ge(silu_done, tile + 1 + OFF)
                dve.tensor_tensor(ac[:], ac[:], pair[0][:, FF:], ALU.mult).then_inc(hid_done, 1)
                if not final:
                    rest_x(tile + 1, 1 - s)
                dve.wait_ge(ah_done, tile + 1 + OFF)
                dve.scalar_tensor_tensor(at_lo[:].rearrange("p k q -> p (k q)"), pair[2][:, 0:FF], 0.5,
                                         at_hi[:].rearrange("p k q -> p (k q)").bitcast(F32),
                                         ALU.mult, ALU.subtract).then_inc(al_done, 1)
                if not final:
                    split_lo_moe(((par + 1) % 2, q + 3))

            dve.wait_ge(route_done, 1)
            last_pair = last_pair_of_tiles(dve)
            split_lo_moe((NB % 2, 0))
            rest_x(0, 0)
            with dve.Fori(0, last_pair) as i:
                for s in range(2):
                    dve_tile(i, s, False)
            dve_tile(last_pair, 0, False)
            dve_tile(last_pair, 1, True)
            dve.wait_ge(s7_in, 64)
            for tt in range(NT):
                cnd = 0 if tt == PROMPT else 1
                y = ya[:, tt % 2]
                dve.wait_ge(y_in[tt % 2], 32 * (tt // 2 + 1))
                link(dve.tensor_scalar(y, y, pair_w[:, tt, 0:1], None, ALU.mult))
                link(dve.scalar_tensor_tensor(y, yc[:, tt % 2], pair_w[:, tt, 1:2], y, ALU.mult, ALU.add))
                link(dve.tensor_tensor(y, y, g2[:, cnd], ALU.mult))
                dve.wait_ge(x7_in[tt % 2], 16 * (tt // 2 + 1))
                link(dve.scalar_tensor_tensor(y, xq[:, tt % 2], ALPHA, y, ALU.mult, ALU.add))
                row_norm(y, y, (f_done, tt + 1))

        @block.tensor
        def _(pe):
            def wait_bank(n):
                if n >= 4:
                    pe.wait_ge(pj_free[n % 4], n // 4)

            def wait_turned(n):
                if n >= 2:
                    pe.wait_ge(tr_free[n % 2], n // 2)

            def project(i):
                kind, b, ci, tt = units[i]
                if b is None:
                    return
                n = pj_no[i]
                wait_bank(n)
                if first_of_block(i):
                    pe.wait_ge(lo_done, NC_CH * (b + 1))
                for kk in range(KD):
                    hi, lo = w_hi[:, b % 2, kk // 2, kk % 2], w_lo[:, b % 2, kk // 2, kk % 2]
                    first, end = kk == 0, kk == KD - 1
                    if kind == "ada":
                        pe.matmul(bank(n)[0:4], cond_hl[:, kk], hi, start=first, stop=False)
                        last = pe.matmul(bank(n)[0:4], cond_hl[:, kk], lo, start=False, stop=end)
                    else:
                        a_hi, a_lo = h_hi[:, kk, tt * P:(tt + 1) * P], h_lo[:, kk, tt * P:(tt + 1) * P]
                        pe.matmul(bank(n), a_hi, hi, start=first, stop=False)
                        pe.matmul(bank(n), a_hi, lo, start=False, stop=False)
                        last = pe.matmul(bank(n), a_lo, hi, start=False, stop=end)
                last.then_inc(pj_ready, 1)

            def turn(i):
                kind, b, ci, tt = units[i]
                if kind == "ada":
                    n = tr_no[i][0]
                    wait_turned(n)
                    pe.wait_ge(pj_free[pj_no[i] % 4], pj_no[i] // 4 + 1)
                    pe.wait_ge(stage5_in[ci % 2], 16 * (ci // 2 + 1))
                    if ci < 4:
                        for j in range(4):
                            last = pe.matmul(turned(n)[:, 2 * j:2 * j + 2], stage5[:, ci % 2, j * P:(j + 1) * P],
                                             pick_cols[:], start=j == 0, stop=True, skip_group_check=True)
                    else:
                        last = pe.matmul(turned(n)[0:2, 0:CW], pick_cols[:], stage5[:, ci % 2], start=True, stop=True)
                    last.then_inc(tr_ready, 1)
                    return
                if i not in hl_no:
                    return
                s = hl_no[i] % 2
                pe.wait_ge(hl_done, hl_no[i] + 1)
                n = tr_no[i][0]
                wait_turned(n)
                for m in range(B_KV if kind in ("bkv", "cbk") else 8):
                    src = hl[:, s, m].rearrange("p h d -> p (h d)")
                    last = pe.transpose(turned(n)[:, m * P:(m + 1) * P], src.bitcast(F32), ident[:])
                last.then_inc(tr_ready, 1)

            pe.wait_ge(cond_silu, 2)
            pe.wait_ge(const_in, 48)
            for i in range(N_EARLY):
                project(i)
                if i:
                    turn(i - 1)
            turn(N_EARLY - 1)
            pe.wait_ge(norm_done, NT)
            for k in range(KD):
                n = H_GROUP0 + k
                wait_turned(n)
                for tt in range(NT):
                    last = pe.transpose(turned(n)[:, tt * P:(tt + 1) * P], x5[:, tt, k * P:(k + 1) * P], ident[:])
                last.then_inc(tr_ready, 1)
            pe.wait_ge(h_done, KD)
            for i in range(N_EARLY, len(units)):
                project(i)
                if i - 2 >= N_EARLY:
                    turn(i - 2)
            turn(len(units) - 2)
            turn(len(units) - 1)
            for i in range(4):
                pe.wait_ge(pj_free[i], (N_PJ + 3 - i) // 4)
            for i in range(2):
                pe.wait_ge(tr_free[i], (N_TR + 1 - i) // 2)

            def scores(m):
                j, n = maps[m]
                bi, kind, r, tt, _ = jobs[j]
                s = bi % 2
                pe.wait_ge(bundle_in[s], 112 * (bi // 2 + 1))
                if m >= 2:
                    pe.wait_ge(e_done, m - 1)
                q = qtb[s][:, r if kind else n, tt * P:(tt + 1) * P]
                k = ktb[s][:, 0 if kind else n]
                runs = [(NKEY, 0, P)] if tt == PROMPT else [(0, 0, CW), (CW, CW, P)]
                for g in range(2):
                    for k0, c0, w in runs:
                        last = pe.matmul(spair(m)[:, c0:c0 + w], q, k[:, g, k0:k0 + w], start=g == 0, stop=g == 1)
                last.then_inc(s_ready, 1)

            def turn_p(j):
                bi, kind, r, tt, m = jobs[j]
                pe.wait_ge(*((e_done, m + 1) if kind else (a_done, j + 1)))
                if j:
                    pe.wait_ge(pt_full[(j - 1) % 2], (j - 1) // 2 + 1)
                src = pbuf[:, m % PR] if kind else abuf[:, j % 2]
                for k in range(width(j) // P):
                    last = pe.transpose(pair[2][:, k * P:(k + 1) * P], src[:, k * P:(k + 1) * P], ident[:])
                last.then_inc(t_ready, 1)

            def times_v(j):
                bi, kind, r, tt, m = jobs[j]
                pe.wait_ge(pt_full[j % 2], j // 2 + 1)
                if j >= 2:
                    pe.wait_ge(o_out, j - 1)
                tiles = [PROMPT] if tt == PROMPT else list(range(TL)) + [NT]
                w = HD if kind else P
                for k, vt in enumerate(tiles):
                    last = pe.matmul(obank(j)[:, 0:w], ptb[:, j % 2, k], vb[bi % 2][:, vt, 0:w], start=k == 0, stop=k == len(tiles) - 1)
                last.then_inc(pv_ready, 1)

            for j in range(NJ + 3):
                if j < NJ:
                    scores(jobs[j][4])
                if 0 <= j - 2 < NJ:
                    turn_p(j - 2)
                if j < NJ and not jobs[j][1]:
                    scores(jobs[j][4] + 1)
                if 0 <= j - 3 < NJ:
                    times_v(j - 3)
            pe.wait_ge(o_out, NJ)
            pe.wait_ge(e_done, NM)

            def turn_rows(n, src):
                wait_turned(n)
                for k in range(KD):
                    last = pe.transpose(turned(n)[:, k * P:(k + 1) * P], src[:, k * P:(k + 1) * P], ident[:])
                last.then_inc(tr_ready, 1)

            def turn_o(z):
                if z >= 2 * NT:
                    return
                if z < NT:
                    pe.wait_ge(on_done, z + 1)
                else:
                    pe.wait_ge(o_in[z % 2], 16 * (z // 2 + 1))
                turn_rows(TR_O + z, oin[:, z % 2])

            def turn_merged(tt):
                pe.wait_ge(mg_done, 3 * NT + tt + 1)
                turn_rows(TR_M + tt, rows[:, tt])

            def three_passes(out, a_hi, a_lo, b, nk):
                for kk in range(nk):
                    hi, lo = w_hi[:, b % 2, kk // 2, kk % 2], w_lo[:, b % 2, kk // 2, kk % 2]
                    pe.matmul(out, a_hi[:, kk], hi, start=kk == 0, stop=False)
                    pe.matmul(out, a_hi[:, kk], lo, start=False, stop=False)
                    last = pe.matmul(out, a_lo[:, kk], hi, start=False, stop=kk == nk - 1)
                return last

            turn_o(0)
            for v in range(4 * NT):
                n, tt, b, br = N_PJ + v, v % NT, branch_block(v), (v // NT) % 2
                turn_o(v + 1)
                wait_bank(n)
                pe.wait_ge(lo_done, NC_CH * (b + 1))
                if v < 2 * NT:
                    pe.wait_ge(tr_free[(TR_O + v) % 2], (TR_O + v) // 2 + 1)
                cols = slice(tt * P, (tt + 1) * P)
                three_passes(bank(n), ot_hi[br][:, :, cols], ot_lo[br][:, :, cols], b, KD).then_inc(pj_ready, 1)
                if v >= 3 * NT + 1:
                    turn_merged(v - 3 * NT - 1)
            turn_merged(NT - 1)
            pe.wait_ge(s4b_in, 14 * 16)
            for tt in range(NT + 2):
                if tt < NT:
                    for h in range(2):
                        n = tail_no["wo", tt, h]
                        b = NB - 2 + h
                        wait_bank(n)
                        pe.wait_ge(lo_done, NC_CH * (b + 1))
                        pe.wait_ge(tr_free[(TR_M + tt) % 2], (TR_M + tt) // 2 + 1)
                        cols = slice(tt * P, (tt + 1) * P)
                        three_passes(bank(n), ot_hi[0][:, :, cols], ot_lo[0][:, :, cols], b, KD).then_inc(pj_ready, 1)
                if tt >= 2:
                    q = tt - 2
                    pe.wait_ge(h2_done, q + 1)
                    turn_rows(TR_H + q, rows[:, q])
                    n = tail_no["L", q]
                    wait_bank(n)
                    pe.wait_ge(tr_free[(TR_H + q) % 2], (TR_H + q) // 2 + 1)
                    for k in range(KD):
                        last = pe.matmul(bank(n)[:, 0:NG + NE], h2t[:, k], w_rt[:, k], start=k == 0, stop=k == KD - 1)
                    last.then_inc(pj_ready, 1)
            pe.wait_ge(mask_done, 1)
            pe.wait_ge(ones_done, 1)
            for i in range(4):
                pe.wait_ge(pj_free[i], (N_PJ2 + 3 - i) // 4)
            for i in range(2):
                pe.wait_ge(tr_free[i], (N_TR2 + 1 - i) // 2)
            for tt in range(NT + 1):
                out = pair[0][:, tt * NE:(tt + 1) * NE]
                for q in range(min(tt + 1, NT)):
                    last = pe.matmul(out, before[:] if q == tt else ones[:], mask[:, q], start=q == 0,
                                     stop=q == min(tt, NT - 1), skip_group_check=True)
            last.then_inc(pre_done, 1)
            for sm in (x_turned, moe_blk, aturned):
                pe.nop().then_inc(sm, OFF)

            def turn_x(tile, s, landed):
                pe.wait_ge(xs_in[s], landed)
                for k in range(KD):
                    last = pe.transpose(pair[1][:, k * P:(k + 1) * P], xs[:, s, k * P:(k + 1) * P], ident[:])
                last.then_inc(x_turned, 1)

            def pe_tile(i, s, final):
                tile, q = 2 * i + s, 6 * i + 3 * s
                b = NB + 3 * s
                for r in range(2):
                    pe.wait_ge(lo_done, NC_CH * (NB + q + r + 1))
                    if r == 0:
                        pe.wait_ge(xl_done, tile + 1 + OFF)
                        pe.wait_ge(hid_done, tile + OFF)
                    three_passes(pair[0][:, r * FF:(r + 1) * FF], xt_hi[:, s], xt_lo[:, s], b + r, KD).then_inc(moe_blk, 1)
                if not final:
                    turn_x(tile + 1, 1 - s, 16 * (i + 1 + s))
                pe.wait_ge(hid_done, tile + 1 + OFF)
                for k in range(KF):
                    last = pe.transpose(pair[2][:, k * P:(k + 1) * P], ac[:, k * P:(k + 1) * P], ident[:])
                last.then_inc(aturned, 1)
                pe.wait_ge(lo_done, NC_CH * (NB + q + 3))
                pe.wait_ge(al_done, tile + 1 + OFF)
                pe.wait_ge(y_copied, tile + OFF)
                for h in range(2):
                    for kk in range(KF):
                        c = kk // 2 + 2 * h
                        hi, lo = w_hi[:, b % 2, c, kk % 2], w_lo[:, b % 2, c, kk % 2]
                        out = pair[3][:, h * CW:(h + 1) * CW]
                        pe.matmul(out, at_hi[:, kk], hi, start=kk == 0, stop=False)
                        pe.matmul(out, at_hi[:, kk], lo, start=False, stop=False)
                        last = pe.matmul(out, at_lo[:, kk], hi, start=False, stop=kk == KF - 1)
                last.then_inc(moe_blk, 1)

            pe.wait_ge(route_done, 1)
            last_pair = last_pair_of_tiles(pe)
            turn_x(0, 0, 16)
            with pe.Fori(0, last_pair) as i:
                for s in range(2):
                    pe_tile(i, s, False)
            pe_tile(last_pair, 0, False)
            pe_tile(last_pair, 1, True)

        @block.gpsimd
        def _(pool):
            def load_bundle(bi):
                kind, h = bundles[bi]
                s, done = bi % 2, bundle_in[bi % 2]
                nq, nk, w = (REP, 1, HD) if kind else (2, 2, P)
                mq, mk = (MAPS_A + REP * h, MAPS_A + h) if kind else (2 * h, 2 * h)
                pool.dma_start(qtb[s][:, 0:nq].bitcast(F32), q_scr[mq:mq + nq].rearrange("m p q -> p m q")).then_inc(done, 16)
                for g in range(2):
                    for part in range(2):
                        pool.dma_start(ktb[s][HD * part:HD * part + HD, 0:nk, g].bitcast(F32),
                                       k_scr[mk:mk + nk, HD * g:HD * g + HD].rearrange("m p q -> p m q")).then_inc(done, 16)
                scr = (vb_scr if kind else va_scr)[:, :, w * h:w * h + w]
                cached = t["cache_b_v"][0, 0, :, h] if kind else t["cache_a_v"][0, 0, :, h]
                pool.dma_start(vb[s][:, 0:NT, 0:w], scr).then_inc(done, 16)
                pool.dma_start(vb[s][:, NT, 0:w], cached).then_inc(done, 16)

            def bias(ci):
                if ci >= 2:
                    prev = [q for q, u in enumerate(units) if u[0] == "ada" and u[2] == ci - 2][0]
                    pool.wait_ge(tr_ready, tr_no[prev][0] + 1)
                pool.dma_start(stage5[4:5, ci % 2], t["b_ada"][0:1, ci * CW:(ci + 1) * CW]).then_inc(stage5_in[ci % 2], 16)

            def store_values(i):
                kind, b, ci, tt = units[i]
                n, j = pj_no[i], vst_no[i]
                if kind == "bkv":
                    pool.wait_ge(v_out, sum(u[0] == "bkv" for u in units[:i + 1]))
                else:
                    pool.wait_ge(pj_free[n % 4], n // 4 + 1)
                s, st = vst[:, j % 2], vst_st[j % 2]
                if kind == "g":
                    pool.dma_start(gate_scr[tt, :, (ci - 9) * CW:(ci - 8) * CW], s).then_inc(st, 16)
                elif kind == "v":
                    c0 = (ci - 4) * CW
                    pool.dma_start(va_scr[:, tt, c0:c0 + CW], s).then_inc(st, 16)
                    if tt == PROMPT:
                        pool.dma_start(t["new_a_v"][0, 0].rearrange("s h d -> s (h d)")[:, c0:c0 + CW],
                                       s).then_inc(st, 16)
                else:
                    pool.dma_start(vb_scr[:, tt], s[:, 0:256]).then_inc(st, 16)
                    if tt == PROMPT:
                        pool.dma_start(t["new_b_v"][0, 0].rearrange("s h d -> s (h d)"), s[:, 0:256]).then_inc(st, 16)

            def store_prompt_k(i):
                kind, b, ci, tt = units[i]
                s = pst_no[i]
                if kind == "k":
                    pool.wait_ge(pj_free[pj_no[i] % 4], pj_no[i] // 4 + 1)
                    dst = t["new_a_k"][0, 0].rearrange("s h n d -> s (h n d)")[:, (ci - 2) * CW:(ci - 1) * CW]
                    pool.dma_start(dst, pst[:, s % 2]).then_inc(pst_st[s % 2], 16)
                else:
                    pool.wait_ge(hl_done, hl_no[i] + 1)
                    pool.dma_start(t["new_b_k"][0, 0].rearrange("s h d -> s (h d)"),
                                   pst[:, s % 2, 0:256]).then_inc(pst_st[s % 2], 16)

            def store_turned(i):
                kind, b, ci, tt = units[i]
                j, n = tst_no[i][0], tr_no[i][0]
                pool.wait_ge(tr_free[n % 2], n // 2 + 1)
                st = tst_st[j % TST]
                if kind in ("q", "bq"):
                    m0, nm = (8 * ci if kind == "q" else MAPS_A + 8 * (ci - 6)), 8
                    dst = q_scr[m0:m0 + nm, :, tt * P:(tt + 1) * P]
                else:
                    m0, nm = {"k": (8 * (ci - 2), 8), "ck": (8 * ci, 8)}.get(kind, (MAPS_A, B_KV))
                    dst = k_scr[m0:m0 + nm, :, key_col(tt):key_col(tt) + P]
                pool.dma_start(dst.rearrange("m p q -> p m q"), tst[:, j % TST, 0:nm]).then_inc(st, 16)

            def after(i):
                kind, b, ci, tt = units[i]
                if i in tst_no:
                    store_turned(i)
                if i in ms_no:
                    n, m = tr_no[i][0], ms_no[i]
                    pool.wait_ge(tr_free[n % 2], n // 2 + 1)
                    pool.dma_start(mod_scr[:, ci * CW:(ci + 1) * CW], mst[:, m % 2]).then_inc(ms_st[m % 2], 16)
                if kind == "ada" and ci + 2 < 12:
                    bias(ci + 2)

            bias(0)
            bias(1)
            for i in range(N_EARLY):
                after(i)
            first_g = [i for i, u in enumerate(units) if u[0] == "g"][0]
            for i in range(N_EARLY, len(units)):
                if i == first_g:
                    for s in range(2):
                        pool.wait_ge(vst_st[s], max(vst_sum[j] for q, j in vst_no.items() if q < i and j % 2 == s))
                if i in vst_no:
                    store_values(i)
                if i in pst_no:
                    store_prompt_k(i)
                if i - 2 >= N_EARLY:
                    after(i - 2)
                if i == first_g + 2:
                    for s in range(TST):
                        pool.wait_ge(tst_st[s], tst_total[s])
                    load_bundle(0)
            after(len(units) - 2)
            after(len(units) - 1)
            pool.wait_ge(pj_ready, N_PJ)
            pool.wait_ge(h_done, KD)
            for i in range(TST):
                pool.wait_ge(tst_st[i], tst_total[i])
            for i in range(2):
                pool.wait_ge(vst_st[i], vst_total[i])
                pool.wait_ge(pst_st[i], 16 * ((N_PST + 1 - i) // 2))
                pool.wait_ge(ms_st[i], 16 * (N_MS // 2))
            for i, name in enumerate(("lambda_q1", "lambda_k1", "lambda_q2", "lambda_k2")):
                pool.dma_start(lam_in[:, i], t[name][0:1, :].to_broadcast([P, HD])).then_inc(lam_in_s, 16)
            load_bundle(1)
            for bi, (kind, h) in enumerate(bundles):
                pool.wait_ge(o_out, job_end[bi])
                c0, w = (D + 2 * P * h, 2 * P) if kind else (P * h, P)
                pool.dma_start(o_scr[:, :, c0:c0 + w].rearrange("t p c -> p t c"), ost[:, bi % 2, :, 0:w]).then_inc(o_st[bi % 2], 16)
                if bi + 2 < len(bundles):
                    load_bundle(bi + 2)
            for i in range(2):
                pool.wait_ge(o_st[i], 16 * (len(bundles) // 2))
            pool.dma_start(gcol[:], t["a_subln_g"][0].rearrange("(d o) -> d o", o=1)).then_inc(gcol_in, 16)

            def load_o(z):
                if z >= 2:
                    pool.wait_ge(tr_ready, TR_O + z - 1)
                tt, c0 = z % NT, (z // NT) * D
                pool.dma_start(oin[:, z % 2], o_scr[tt, :, c0:c0 + D]).then_inc(o_in[z % 2], 16)

            def load_gate(v):
                if v >= 2:
                    pool.wait_ge(mg_done, v - 1)
                c0 = (v // NT % 2) * D + (v // (2 * NT)) * CW
                pool.dma_start(gin[:, v % 2], gate_scr[v % NT, :, c0:c0 + CW]).then_inc(g_in[v % 2], 16)

            load_o(0)
            load_o(1)
            load_gate(0)
            load_gate(1)
            for v in range(4 * NT - 2):
                if v + 2 < 2 * NT:
                    load_o(v + 2)
                load_gate(v + 2)
                if v == 0:
                    pool.wait_ge(zero_done, 1)
                for i in range(2 * v, min(2 * v + 2, TILES)):
                    pool.dma_start(slots_scr[i * P:(i + 1) * P], zero[:]).then_inc(zero_st, 16)
            pool.wait_ge(mg_done, 4 * NT)
            pool.wait_ge(pj_ready, N_PJ + 4 * NT)
            for i in range(2):
                pool.dma_start(ln1[:, i], t["ln1_b" if i else "ln1_g"][0:1, :].to_broadcast([P, D])).then_inc(s4b_in, 16)
            for cnd in range(2):
                for i, m in enumerate((2, 3, 4)):
                    pool.dma_start(bc[:, cnd, i], mod_scr[cnd:cnd + 1, m * D:(m + 1) * D].to_broadcast([P, D])).then_inc(s4b_in, 16)
            pool.dma_start(before[:], t["k_before"]).then_inc(s4b_in, 16)
            pool.dma_start(tab[:], t["k_tab"][0:1, :].to_broadcast([P, TAB_W])).then_inc(s4b_in, 16)
            for w, b, c0, c1 in (("w_coarse", "b_coarse", 0, NG), ("w_fine", "b_fine", NG, NG + NE)):
                pool.dma_start(w_rt[:, :, c0:c1], t[w][0].rearrange("(k p) n -> p k n", p=P)).then_inc(s4b_in, 16)
                pool.dma_start(b_rt[:, c0:c1], t[b][0:1, :].to_broadcast([P, c1 - c0])).then_inc(s4b_in, 16)

            def load_x(tt):
                if tt >= 2:
                    pool.wait_ge(ya_done, tt - 1)
                src = t["x_prompt"][0] if tt == PROMPT else t["x_sample"][0, tt * P:(tt + 1) * P]
                pool.dma_start(xr[:, tt % 2], src).then_inc(x4_in[tt % 2], 16)

            load_x(0)
            load_x(1)
            pool.wait_ge(s4b_in, 14 * 16)
            for tt in range(NT + 1):
                if tt < NT:
                    pool.wait_ge(ya_done, tt + 1)
                    if tt + 2 < NT:
                        load_x(tt + 2)
                    y = yb[:, tt % 2]
                    pool.tensor_tensor(y, y, ln1[:, 0], ALU.mult).then_inc(x1_part, 1)
                    pool.wait_ge(x1_part, tt + 1)
                    pool.tensor_tensor(y, y, ln1[:, 1], ALU.add).then_inc(x1_done, 1)
                    pool.wait_ge(x1_done, tt + 1)
                    pool.dma_start(x1_scr[tt], y).then_inc(x1_st[tt % 2], 16)
                if tt:
                    q = tt - 1
                    cnd = 0 if q == PROMPT else 1
                    pool.wait_ge(yb_done, q + 1)
                    pool.wait_ge(bc_done, 1)
                    pool.tensor_tensor(rows[:, q], rows[:, q], bc[:, cnd, 2], ALU.mult).then_inc(h2_part, 1)
                    pool.wait_ge(h2_part, q + 1)
                    pool.tensor_tensor(rows[:, q], rows[:, q], bc[:, cnd, 1], ALU.add).then_inc(h2_done, 1)
            pool.wait_ge(x1_st[0], 48)
            pool.wait_ge(x1_st[1], 32)
            pool.wait_ge(route_done, 1)
            pool.wait_ge(zero_st, 16 * TILES)
            for tt in range(NT):
                for c in range(2):
                    pool.indirect_dma_start(out=slots_scr, out_offset=bass.IndirectOffsetOnAxis(ap=slot_i[:, tt, c:c + 1], axis=0),
                                            in_=rows[:, tt], in_offset=None).then_inc(scat_st, 16)
            last_pair = last_pair_of_tiles(pool)
            pool.nop().then_inc(y_free, OFF)
            pool.wait_ge(scat_st, 16 * 2 * NT)
            slot_tiles = slots_scr.rearrange("(n p) c -> n p c", p=P)
            pool.dma_start(xs[:, 0], slot_tiles[0]).then_inc(xs_in[0], 16)
            pool.dma_start(xs[:, 1], slot_tiles[1]).then_inc(xs_in[1], 16)

            def pool_tile(i, s, final):
                tile = 2 * i + s
                if not final:
                    pool.wait_ge(x_turned, tile + 1 + OFF)
                    pool.dma_start(xs[:, s], slot_tiles[bass.ds(tile + 2, 1)].rearrange("o p c -> (o p) c")).then_inc(xs_in[s], 16)
                pool.wait_ge(y_copied, tile + 1 + OFF)
                pool.dma_start(slot_tiles[bass.ds(tile, 1)].rearrange("o p c -> (o p) c"), yo[:, s]).then_inc(y_st[s], 16)
                pool.wait_ge(y_st[s], 16 * (i + 1))
                pool.nop().then_inc(y_free, 1)

            with pool.Fori(0, last_pair) as i:
                for s in range(2):
                    pool_tile(i, s, False)
            pool_tile(last_pair, 0, True)
            pool_tile(last_pair, 1, True)
            for c in range(2):
                pool.dma_start(g2[:, c], mod_scr[c:c + 1, 5 * D:6 * D].to_broadcast([P, D])).then_inc(s7_in, 16)
                pool.dma_start(ln2[:, c], t["ln2_b" if c else "ln2_g"][0:1, :].to_broadcast([P, D])).then_inc(s7_in, 16)

            def gather(tt):
                s = tt % 2
                for c, dst in enumerate((ya, yc)):
                    pool.indirect_dma_start(out=dst[:, s], out_offset=None, in_=slots_scr,
                                            in_offset=bass.IndirectOffsetOnAxis(ap=slot_i[:, tt, c:c + 1], axis=0)).then_inc(y_in[s], 16)
                pool.dma_start(xq[:, s], x1_scr[tt]).then_inc(x7_in[s], 16)

            gather(0)
            gather(1)
            pool.wait_ge(s7_in, 64)
            for tt in range(NT):
                s = tt % 2
                pool.wait_ge(f_done, tt + 1)
                pool.tensor_tensor(ya[:, s], ya[:, s], ln2[:, 0], ALU.mult).then_inc(fg_done, 1)
                pool.wait_ge(fg_done, tt + 1)
                pool.tensor_tensor(ya[:, s], ya[:, s], ln2[:, 1], ALU.add).then_inc(fb_done, 1)
                pool.wait_ge(fb_done, tt + 1)
                dst = t["y_prompt"][0] if tt == PROMPT else t["y_sample"][0, tt * P:(tt + 1) * P]
                pool.dma_start(dst, ya[:, s]).then_inc(out_st[s], 16)
                if tt + 2 < NT:
                    pool.wait_ge(out_st[s], 16 * (tt // 2 + 1))
                    gather(tt + 2)
            pool.wait_ge(out_st[0], 48)
            pool.wait_ge(out_st[1], 32)
            for s in range(2):
                pool.wait_ge(vst_st[s], vst_total[s])
                pool.wait_ge(ms_st[s], 16 * (N_MS // 2))
                pool.wait_ge(pst_st[s], 16 * ((N_PST + 1 - s) // 2))


_INS = ["x_prompt", "x_sample", "cache_a_k", "cache_a_v", "cache_b_k", "cache_b_v", "w_ada", "b_ada",
        "w_in", "lambda_q1", "lambda_k1", "lambda_q2", "lambda_k2", "a_subln_g", "b_q_g", "b_k_g", "w_br_a", "w_br_b",
        "w_o", "ln1_g", "ln1_b", "w_coarse", "b_coarse", "w_fine", "b_fine", "w_gate_up", "w_down", "ln2_g", "ln2_b"]
_OUTS = [("y_prompt", (1, N_CTX, D)), ("y_sample", (1, N_LAT, D)), ("new_a_k", (1, 1, N_CTX, A_HEADS, 2, HD)),
         ("new_a_v", (1, 1, N_CTX, A_HEADS, 2 * HD)), ("new_b_k", (1, 1, N_CTX, B_KV, HD)),
         ("new_b_v", (1, 1, N_CTX, B_KV, HD))]


def shape_constants():
    f = np.float32
    half = HD // 2
    freqs = (f(10000.0) ** (-np.arange(0, half, 2, dtype=f) / f(half))).astype(f)
    rows = np.repeat(np.arange(N_LAT // GRID_W, dtype=f), GRID_W)
    cols = np.tile(np.arange(GRID_W, dtype=f), N_LAT // GRID_W)
    ang = np.concatenate([rows[:, None] * freqs, cols[:, None] * freqs], -1).astype(f)
    pick = np.array([[1, 0], [0, 1], [1, 0], [0, 1], [1, 1]], f)
    return {
        "k_ident": np.eye(P, dtype=f),
        "k_pick": pick,
        "k_cos": np.repeat(np.cos(ang).astype(f), 2, axis=1),
        "k_sin": np.sin(ang).astype(f),
        "k_nsin": (-np.sin(ang)).astype(f),
        "k_before": np.triu(np.ones((P, P), f), 1),
        "k_tab": np.concatenate([np.tril(np.ones((NE, NE), f)).ravel(), P * np.arange(NE, dtype=f), f([4, 3, 2, 1]),
                                 2 * np.arange(MORE // 2, dtype=f), np.arange(TILES, dtype=f),
                                 np.arange(MORE, dtype=f)]).reshape(1, TAB_W),
    }


def kernel(**inputs):
    import concourse.bacc as bacc
    from concourse.bass_utils import run_bass_kernel_spmd

    nc = bacc.Bacc("TRN2", target_bir_lowering=False, num_devices=1)
    arrays, t = {}, {}
    for name in _INS:
        arrays[f"in_{name}"] = np.ascontiguousarray(inputs[name])
    conds = np.stack([np.asarray(inputs["c_ctx"]), np.asarray(inputs["c"])[0]], axis=-1)
    arrays["in_conds"] = np.ascontiguousarray(conds.reshape(KD, P, 2).transpose(1, 0, 2))
    for name, a in shape_constants().items():
        arrays[f"in_{name}"] = np.ascontiguousarray(a)
    for name, a in arrays.items():
        t[name[3:]] = nc.dram_tensor(name, a.shape, mybir.dt.from_np(a.dtype), kind="ExternalInput").ap()
    for name, shape in _OUTS:
        t[name] = nc.dram_tensor(f"out_{name}", shape, F32, kind="ExternalOutput").ap()
    hybrid_step(nc, t)
    r = run_bass_kernel_spmd(nc, [arrays], core_ids=[0])
    return tuple(r.results[0][f"out_{name}"] for name, _ in _OUTS)
```

```python
import math
from contextlib import ExitStack

import numpy as np

import concourse.bass as bass
from concourse import mybir

F32 = mybir.dt.float32
F32R = mybir.dt.float32r
I32 = mybir.dt.int32
U32 = mybir.dt.uint32
ACT = mybir.ActivationFunctionType
ALU = mybir.AluOpType
AX = mybir.AxisListType

P = 128
D = 1024
KD = D // P
N_LAT = 512
N_CTX = 128
TL = N_LAT // P
NT = TL + 1
PROMPT = TL
GRID_W = 64
HD = 64
A_HEADS = 8
B_HEADS = 16
B_KV = 4
REP = B_HEADS // B_KV
NE = 16
NG = 4
EPG = NE // NG
FF = 512
KF = FF // P
EPS = 1e-5
ALPHA = 2 ** 0.25
SCALE = HD ** -0.5
LAMBDA_INIT = 0.8 - 0.6 * math.exp(0.0)
CW = 512
NC_CH = 4
NKEY = N_LAT + N_CTX
KCOL = NKEY + P
RSQRT_MAGIC = 0x5F3759DF
MAPS_A = 2 * A_HEADS
PAIRS = 2 * P * NT
OVER = (PAIRS - NE) // P
TILES = NE + OVER + (NE + OVER) % 2
MORE = TILES - NE
T_TRI, T_ROW, T_PRI, T_PAIR, T_TILE, T_MORE = np.cumsum([0, NE * NE, NE, NG, MORE // 2, TILES]).tolist()
TAB_W = T_MORE + MORE
OFF = 3


def rsqrt(dve, link, y, v, half, shifted):
    link(dve.tensor_scalar(shifted, v.bitcast(I32), 1, None, ALU.logical_shift_right))
    link(dve.tensor_scalar(y.bitcast(I32), shifted, -1.0, float(RSQRT_MAGIC), ALU.mult, ALU.add))
    for _ in range(3):
        link(dve.tensor_tensor(half, y, y, ALU.mult))
        link(dve.scalar_tensor_tensor(half, half, -0.5, v, ALU.mult, ALU.mult))
        link(dve.scalar_tensor_tensor(y, half, 1.5, y, ALU.add, ALU.mult))


def chain(eng, sem):
    count = [0]

    def link(ins):
        count[0] += 1
        ins.then_inc(sem, 1)
        eng.wait_ge(sem, count[0])

    return link


def over(ap, n, shape):
    return ap.unsqueeze(n).to_broadcast(shape)


def hybrid_step(nc, t):
    with ExitStack() as ctx:
        def sb(name, shape, dt=F32, stack=ctx):
            return stack.enter_context(nc.sbuf_tensor(name, shape, dt))

        def sem(name):
            return ctx.enter_context(nc.semaphore(name))

        def dram(name, shape, dt=F32):
            return nc.dram_tensor(name, shape, dt, kind="Internal").ap()

        pair = [ctx.enter_context(nc.psum_tensor(f"psum_pair{i}", [P, 2 * CW], F32)) for i in range(4)]

        q_scr = dram("q_transposed", (MAPS_A + B_HEADS, P, NT * P))
        k_scr = dram("k_transposed", (MAPS_A + B_KV, P, KCOL))
        va_scr = dram("values_a", (P, NT, D))
        vb_scr = dram("values_b", (P, NT, B_KV * HD))
        gate_scr = dram("gate_tanh", (NT, P, 2 * D))
        mod_scr = dram("modulation", (2, 6 * D))
        o_scr = dram("attention_out", (NT, P, 2 * D))
        x1_scr = dram("x_after_ln1", (NT, P, D))
        slots_scr = dram("expert_rows", ((TILES + 1) * P, D))

        ident = sb("identity", [P, P])
        pick_cols = sb("pick_cols", [5, 2])
        eps_row = sb("half_tiles", [P, 8])
        cond = sb("cond", [P, KD, 2])
        cond_t = sb("cond_tanh", [P, KD, 2])
        cond_hl = sb("cond_hi_lo", [P, KD, 4], F32R)
        mod_t = sb("mod_transposed", [P, 2 * KD, 2])
        lam_in = sb("lambda_vectors", [P, 4, HD])
        lam_s = sb("lambda_sums", [P, 2])
        lam_e = sb("lambda_exps", [P, 2])
        nlam = sb("minus_lambda", [P, 1])
        w_raw = sb("w_raw", [P, NC_CH, 2, CW])
        w_hi = sb("w_hi", [P, 2, NC_CH, 2, CW], F32R)
        w_lo = sb("w_lo", [P, 2, NC_CH, 2, CW], F32R)

        raw_in = [sem(f"w_raw_in{c}") for c in range(NC_CH)]
        hi_done = sem("w_hi_done")
        lo_done = sem("w_lo_done")
        const_in = sem("const_in")
        lam_in_s = sem("lambda_in")
        x_in = sem("x_in")
        dve_link = sem("dve_link")
        act_link = sem("act_link")
        pj_ready = sem("proj_ready")
        pj_free = [sem(f"proj_free{i}") for i in range(4)]
        tr_ready = sem("turned_ready")
        tr_free = [sem(f"turned_free{i}") for i in range(2)]

        w_ada = t["w_ada"][0].rearrange("(k p) n -> p k n", p=P)
        w_in = t["w_in"][0].rearrange("(k p) n -> p k n", p=P)
        w_br = {"wa": t["w_br_a"][0].rearrange("(k p) n -> p k n", p=P),
                "wb": t["w_br_b"][0].rearrange("(k p) n -> p k n", p=P),
                "wo": t["w_o"][0].rearrange("(k p) n -> p k n", p=P)}
        blocks = [("ada", i) for i in range(4)]
        for i in range(13):
            blocks.append(("in", i))
            if i < 8:
                blocks.append(("ada", 4 + i))
        blocks += [("wa", 0), ("wb", 0), ("wa", 1), ("wb", 1), ("wo", 0), ("wo", 1)]
        NB = len(blocks)

        def block_chunk(b, c):
            kind, i = blocks[b]
            src = w_ada if kind == "ada" else w_in if kind == "in" else w_br[kind]
            return src[:, 2 * c:2 * c + 2, i * CW:(i + 1) * CW]

        KINDS = ["q", "q", "k", "k", "v", "v", "bq", "bq", "bkv", "g", "g", "g", "g"]
        units = []
        for b in range(4, NB - 6):
            kind, i = blocks[b]
            if kind == "ada":
                units.append(("ada", b, i, 0))
            else:
                if i == 2:
                    units += [("ck", None, 0, NT), ("ck", None, 1, NT), ("cbk", None, 0, NT)]
                units += [(KINDS[i], b, i, tt) for tt in range(NT)]
        units = [("ada", b, b, 0) for b in range(4)] + units
        N_EARLY = 4

        pj_no, n = {}, 0
        for i, (kind, b, _, _) in enumerate(units):
            if b is not None:
                pj_no[i] = n
                n += 1
        N_PJ = n
        last_no = {units[i][1]: pj_no[i] for i in sorted(pj_no)}
        GROUPS = {"q": 1, "k": 1, "bq": 1, "bkv": 1, "ck": 1, "cbk": 1, "ada": 1, "v": 0, "g": 0}
        tr_no, n = {}, 0
        for i in range(N_EARLY):
            tr_no[i] = [n]
            n += 1
        H_GROUP0 = n
        n += KD
        for i in range(N_EARLY, len(units)):
            tr_no[i] = list(range(n, n + GROUPS[units[i][0]]))
            n += GROUPS[units[i][0]]
        N_TR = n

        def key_col(tt):
            return {PROMPT: NKEY, NT: N_LAT}.get(tt, tt * P)

        def bank(n):
            return pair[(n % 4) // 2][:, (n % 2) * CW:(n % 2 + 1) * CW]

        def turned(n):
            return pair[2 + n % 2]

        def first_of_block(i):
            return units[i][1] is not None and (i == 0 or units[i - 1][1] != units[i][1]) and not (
                units[i][1] is not None and any(u[1] == units[i][1] for u in units[:i]))

        TST = 3
        tst_no, vst_no, pst_no, hl_no, ms_no = {}, {}, {}, {}, {}
        a = v = p = h = m = 0
        for i, (kind, b, ci, tt) in enumerate(units):
            if kind in ("q", "k", "bq", "bkv", "ck", "cbk"):
                tst_no[i] = list(range(a, a + GROUPS[kind]))
                a += GROUPS[kind]
                hl_no[i] = h
                h += 1
            if kind in ("v", "g", "bkv"):
                vst_no[i] = v
                v += 1
            if kind in ("k", "bkv") and tt == PROMPT:
                pst_no[i] = p
                p += 1
            if kind == "ada" and ci >= 4:
                ms_no[i] = m
                m += 1
        N_TST, N_VST, N_PST, N_MS = a, v, p, m
        hl_users = sorted(hl_no, key=lambda i: hl_no[i])

        tst_st = [sem(f"turned_stored{i}") for i in range(TST)]
        vst_st = [sem(f"values_stored{i}") for i in range(2)]
        pst_st = [sem(f"prompt_k_stored{i}") for i in range(2)]
        ms_st = [sem(f"mod_stored{i}") for i in range(2)]
        tst_sum, vst_sum = {}, {}
        count = [0] * TST
        for i in sorted(tst_no):
            for j in tst_no[i]:
                count[j % TST] += 16
                tst_sum[j] = count[j % TST]
        tst_total = list(count)
        count = [0] * 2
        for i in sorted(vst_no):
            j = vst_no[i]
            count[j % 2] += 32 if units[i][3] == PROMPT and units[i][0] != "g" else 16
            vst_sum[j] = count[j % 2]
        vst_total = list(count)

        stage5_in = [sem(f"bias_in{i}") for i in range(2)]
        cond_silu = sem("cond_silu")
        norm_done = sem("x_normed")
        aff_done = sem("h_affine")
        h_done = sem("h_split")
        sq_done = sem("squares_done")
        v_out = sem("v_staged")
        hl_done = sem("hl_done")
        pst_out = sem("prompt_k_staged")
        cache_in = sem("cache_in")

        s3a = ExitStack()
        bundles = [(0, h) for h in range(A_HEADS)] + [(1, g) for g in range(B_KV)]
        qtb = [sb("q_bundle0", [P, REP, NT * P], F32R, s3a)]
        ktb = [sb("k_bundle0", [P, 2, 2, KCOL], F32R, s3a)]
        vb = [sb("v_bundle0", [P, NT + 1, P], F32, s3a)]
        s12 = ExitStack()
        h_hi = sb("h_hi", [P, KD, NT * P], F32R, s12)
        h_lo = sb("h_lo", [P, KD, NT * P], F32R, s12)
        stage5 = sb("mod_parts", [5, 2, CW], F32, s12)
        cache = sb("cache_k", [P, D + B_KV * HD], F32, s12)
        cosd = sb("rope_cos", [P, TL, HD], F32, s12)
        sind = sb("rope_sin", [P, TL, HD // 2], F32, s12)
        nsin = sb("rope_minus_sin", [P, TL, HD // 2], F32, s12)
        g_q = sb("b_q_gain", [P, HD], F32, s12)
        g_k = sb("b_k_gain", [P, HD], F32, s12)
        s1 = ExitStack()
        x5 = sb("x_tiles", [P, NT, D], F32, s1)
        stats = sb("x_stats", [P, NT, 12], F32, s1)
        mv = sb("x_mean_var", [P, NT, 2], F32, s1)
        var5 = sb("x_var", [P, NT], F32, s1)
        rstd5 = sb("x_rstd", [P, NT], F32, s1)
        half5 = sb("x_half", [P, NT], F32, s1)
        shift5 = sb("x_shift", [P, NT], I32, s1)
        h_mod = sb("h_modulated", [P, 2, NT * P], F32, s1)
        s1.close()
        s2 = ExitStack()
        rt = sb("rope_a", [P, CW], F32, s2)
        ru = sb("rope_b", [P, CW], F32, s2)
        rr = sb("rotated", [P, CW], F32, s2)
        sq = sb("squares", [P, 2, CW], F32, s2)
        qn = sb("normed", [P, CW], F32, s2)
        ms8 = sb("mean_squares", [P, 8], F32, s2)
        rs8 = sb("rms_recip", [P, 8], F32, s2)
        hf8 = sb("rms_half", [P, 8], F32, s2)
        sh8 = sb("rms_shift", [P, 8], I32, s2)
        hl = sb("hi_lo", [P, 2, 8, 2, HD], F32R, s2)
        tst = sb("turned_staging", [P, TST, 8, P], F32, s2)
        vst = sb("value_staging", [P, 2, CW], F32, s2)
        pst = sb("prompt_k_staging", [P, 2, CW], F32, s2)
        mst = sb("mod_staging", [2, 2, CW], F32, s2)
        s2.close()
        s12.close()

        s3 = ExitStack()
        qtb.append(sb("q_bundle1", [P, REP, NT * P], F32R, s3))
        ktb.append(sb("k_bundle1", [P, 2, 2, KCOL], F32R, s3))
        vb.append(sb("v_bundle1", [P, NT + 1, P], F32, s3))
        PR, RR = 4, 16
        pbuf = sb("p_unnormed", [P, PR, NKEY], F32, s3)
        abuf = sb("p_difference", [P, 2, NKEY], F32, s3)
        ptb = sb("p_turned", [P, 2, NT, P], F32, s3)
        ost = sb("o_staging", [P, 2, NT, 2 * P], F32, s3)
        nmax = sb("minus_max", [P, RR], F32, s3)
        rsum = sb("p_sums", [P, RR], F32, s3)
        rinv = sb("p_sums_recip", [P, RR], F32, s3)
        coef = sb("map_coef", [P, 1], F32, s3)
        s3.close()
        s3a.close()

        jobs, maps = [], []
        for bi, (kind, _) in enumerate(bundles):
            for r in range(REP if kind else 1):
                for tt in range(NT):
                    j = len(jobs)
                    jobs.append((bi, kind, r, tt, len(maps)))
                    maps += [(j, 0)] if kind else [(j, 0), (j, 1)]
        NJ, NM = len(jobs), len(maps)
        job_end = {bi: max(j for j, q in enumerate(jobs) if q[0] == bi) + 1 for bi in range(len(bundles))}
        map_end = {bi: max(m for m, q in enumerate(maps) if jobs[q[0]][0] == bi) + 1 for bi in range(len(bundles))}
        first_in = sem("first_bundle_in")
        qk_in = [sem(f"q_k_in{i}") for i in range(2)]
        v_in = [sem(f"v_in{i}") for i in range(2)]
        lam_sem = sem("lambda_steps")
        s_ready = sem("scores_ready")
        nb_done = sem("max_done")
        e_done = sem("exp_done")
        a_done = sem("difference_done")
        t_ready = sem("p_turned_ready")
        pt_full = [sem(f"p_turned_copied{i}") for i in range(2)]
        pv_ready = sem("pv_ready")
        o_out = sem("o_scaled")
        o_st = [sem(f"o_stored{i}") for i in range(2)]

        def spair(m):
            return pair[m % 2]

        def obank(j):
            return pair[3][:, (j % 2) * CW:(j % 2) * CW + P]

        def width(j):
            return P if jobs[j][3] == PROMPT else NKEY

        def copied_by_dve(j):
            return jobs[j][1] == 1 and j % 3 == 0

        def copy_turned(eng, copy, j):
            eng.wait_ge(t_ready, j + 1)
            if j >= 2:
                eng.wait_ge(pv_ready, j - 1)
            w = width(j)
            dst = ptb[:, j % 2].rearrange("p k q -> p (k q)")[:, 0:w]
            copy(dst, pair[2][:, 0:w]).then_inc(pt_full[j % 2], 1)
        def load_qk(eng, bi, done):
            kind, h = bundles[bi]
            s = bi % 2
            nq, nk = (REP, 1) if kind else (2, 2)
            mq, mk = (MAPS_A + REP * h, MAPS_A + h) if kind else (2 * h, 2 * h)
            eng.dma_start(qtb[s][:, 0:nq].bitcast(F32), q_scr[mq:mq + nq].rearrange("m p q -> p m q")).then_inc(done, 16)
            for g in range(2):
                for part in range(2):
                    eng.dma_start(ktb[s][HD * part:HD * part + HD, 0:nk, g].bitcast(F32),
                                  k_scr[mk:mk + nk, HD * g:HD * g + HD].rearrange("m p q -> p m q")).then_inc(done, 16)

        def load_v(eng, bi, done):
            kind, h = bundles[bi]
            s, w = bi % 2, HD if kind else P
            eng.dma_start(vb[s][:, 0:NT, 0:w], (vb_scr if kind else va_scr)[:, :, w * h:w * h + w]).then_inc(done, 16)
            eng.dma_start(vb[s][:, NT, 0:w], t["cache_b_v"][0, 0, :, h] if kind else t["cache_a_v"][0, 0, :, h]).then_inc(done, 16)
        s4 = ExitStack()
        ot_hi = [sb("oA_turned_hi", [P, KD, NT * P], F32R, s4)]
        ot_lo = [sb("oA_turned_lo", [P, KD, NT * P], F32R, s4)]
        rows = sb("rows", [P, NT, D], F32, s4)
        logit = sb("logits", [P, NT, NG + NE], F32, s4)
        slot_i = sb("slot_of_pair", [P, NT, 2], U32, s4)
        pair_w = sb("weight_of_pair", [P, NT, 2], F32, s4)
        ctl = sb("control", [P, 1 + TILES], I32, s4)
        zero = sb("zeros", [P, P], F32, s4)
        st4 = sb("row_stats", [P, 12], F32, s4)
        mv4 = sb("row_mean_var", [P, 2], F32, s4)
        va4 = sb("row_var", [P, 1], F32, s4)
        rs4 = sb("row_rstd", [P, 1], F32, s4)
        hf4 = sb("row_half", [P, 1], F32, s4)
        sh4 = sb("row_shift", [P, 1], I32, s4)
        before = sb("earlier_tokens", [P, P], F32, s4)
        ones = sb("ones", [P, P], F32, s4)
        tab = sb("tables", [P, TAB_W], F32, s4)
        s4a = ExitStack()
        ot_hi.append(sb("oB_turned_hi", [P, KD, NT * P], F32R, s4a))
        ot_lo.append(sb("oB_turned_lo", [P, KD, NT * P], F32R, s4a))
        OS = 3
        oin = sb("o_rows", [P, OS, D], F32, s4a)
        gin = sb("gate_rows", [P, 2, CW], F32, s4a)
        sqb = sb("o_squares", [P, D], F32, s4a)
        gated = sb("gated_b", [P, CW], F32, s4a)
        oms = sb("o_mean_squares", [P, 8], F32, s4a)
        ors = sb("o_rms_recip", [P, 8], F32, s4a)
        ohf = sb("o_half", [P, 8], F32, s4a)
        osh = sb("o_shift", [P, 8], I32, s4a)
        gcol = sb("subln_gain", [P, 1], F32, s4a)
        s4a.close()
        s4b = ExitStack()
        yb = sb("y_rows", [P, 2, D], F32, s4b)
        xr = sb("x_rows", [P, 2, D], F32, s4b)
        ln1 = sb("ln1_gain_bias", [P, 2, D], F32, s4b)
        bc = sb("mod_rows", [P, 2, 3, D], F32, s4b)
        h2t = sb("h2_turned", [P, KD, P], F32, s4b)
        w_rt = sb("router_weights", [P, KD, NG + NE], F32, s4b)
        b_rt = sb("router_bias", [P, NG + NE], F32, s4b)
        s4b.close()
        raw_odd = sb("w_raw_odd", [P, NC_CH, 2, CW], F32, s4)
        s5 = ExitStack()
        mc = sb("coarse_max", [P, NT], F32, s5)
        oh_g = sb("group_pick", [P, NT, NG], F32, s5)
        ex = sb("exp_args", [P, NT, NG + 1], F32, s5)
        ee = sb("exps", [P, NT, NG + 1], F32, s5)
        prod = sb("route_products", [P, NT, NG, EPG], F32, s5)
        fs = sb("fine_logits", [P, NT, EPG], F32, s5)
        m1 = sb("fine_max", [P, NT], F32, s5)
        m2 = sb("fine_second", [P, NT], F32, s5)
        pk = [sb(f"fine_pick{i}", [P, NT, EPG], F32, s5) for i in range(2)]
        pri = sb("pick_priority", [P, NT], F32, s5)
        choice = [sb(f"expert_pick{i}", [P, NT, NG, EPG], F32, s5) for i in range(2)]
        mask = sb("expert_mask", [P, NT, NE], F32, s5)
        den = sb("weight_denom", [P, NT], F32, s5)
        posn = sb("positions", [P, NT + 1, NE], F32, s5)
        sofar = sb("counts_so_far", [P, NE], F32, s5)
        nov = sb("over_tiles", [P, NE], F32, s5)
        tri = sb("over_products", [P, NE, NE], F32, s5)
        ovc = sb("over_cumulated", [P, NE], F32, s5)
        v2 = sb("over_base", [P, NE], F32, s5)
        slotf = sb("slot_numbers", [P, NT, 2], F32, s5)
        cf = sb("control_f", [P, 1 + TILES], F32, s5)
        cle = sb("over_compare", [P, MORE, NE], F32, s5)
        s5.close()
        s6 = ExitStack()
        xs = sb("expert_in", [P, 2, D], F32, s6)
        xt_hi = sb("expert_in_hi", [P, 2, KD, P], F32R, s6)
        xt_lo = sb("expert_in_lo", [P, 2, KD, P], F32R, s6)
        th = sb("gate_tanh_rows", [P, FF], F32, s6)
        ac = sb("expert_hidden", [P, FF], F32, s6)
        at_hi = sb("hidden_hi", [P, KF, P], F32R, s6)
        at_lo = sb("hidden_lo", [P, KF, P], F32R, s6)
        yo = sb("expert_out_rows", [P, 2, D], F32, s6)
        s6.close()
        s7 = ExitStack()
        YS = 3
        ya = sb("first_expert_rows", [P, YS, D], F32, s7)
        yc = sb("second_expert_rows", [P, YS, D], F32, s7)
        xq = sb("x1_rows", [P, YS, D], F32, s7)
        s7.close()

        exp_in = sem("route_exp_in")
        exp_out = sem("route_exp_out")
        ones_done = sem("ones_done")
        mask_done = sem("mask_done")
        pre_done = sem("positions_done")
        route_done = sem("route_done")
        scat_st = sem("rows_scattered")
        xs_in = [sem(f"expert_in{i}") for i in range(2)]
        x_turned = sem("expert_in_turned")
        xh_done = sem("expert_in_hi_done")
        xl_done = sem("expert_in_split")
        moe_used = sem("moe_chunks_used")
        raw2_in = [sem(f"w_raw_odd_in{c}") for c in range(NC_CH)]
        th_done = sem("gate_tanh_done")
        silu_done = sem("silu_done")
        hid_done = sem("hidden_done")
        aturned = sem("hidden_turned")
        ah_done = sem("hidden_hi_done")
        al_done = sem("hidden_split")
        y_copied = sem("expert_out_copied")
        y_st = [sem(f"expert_out_stored{i}") for i in range(2)]
        y_free = sem("expert_out_free")
        s7_in = sem("gate2_in")
        y_in = [sem(f"pair_rows_in{i}") for i in range(YS)]
        x7_in = [sem(f"x1_rows_in{i}") for i in range(YS)]
        w_first = sem("first_rows_weighted")
        f_done = sem("out_normed")
        fg_done = sem("out_scaled")
        fb_done = sem("out_done")
        out_st = [sem(f"out_stored{i}") for i in range(YS)]
        moe_over = sem("moe_over")
        ln2, g2 = rows[:, 0:2], rows[:, 2:4]
        w_gu = t["w_gate_up"][0].rearrange("e (k p) n -> p e k n", p=P)
        w_dn = t["w_down"][0].rearrange("e (k p) n -> p e k n", p=P)


        def landing(q, half, c):
            if q % 2:
                return raw_odd[:, c], raw2_in[c], 16 * (half + 1)
            return w_raw[:, c], raw_in[c], 16 * (NB + half + 1)

        def used(q):
            return NC_CH * q + OFF

        def step_blocks(i, s):
            return [(6 * i + n, n % 2, 3 * i + n // 2) for n in range(3 * s + 2, 3 * s + 5)]

        def expert_chunk(e, r, c):
            if r < 2:
                return w_gu[:, e, 2 * c:2 * c + 2, r * FF:(r + 1) * FF]
            return w_dn[:, e, 2 * (c % 2):2 * (c % 2) + 2, (c // 2) * CW:(c // 2 + 1) * CW]

        def last_pair_of_tiles(eng):
            return eng.value_load(ctl[0:1, 0:1], min_val=NE // 2 - 1, max_val=TILES // 2 - 1)
        s4.close()

        B_WA = NB - 6
        o_in = [sem(f"o_rows_in{i}") for i in range(OS)]
        g_in = [sem(f"gate_rows_in{i}") for i in range(2)]
        gcol_in = sem("subln_gain_in")
        gcol_done = sem("subln_gain_done")
        osq_done = sem("o_squares_done")
        on_done = sem("o_normed")
        oh_done = sem("o_hi_done")
        ot_done = sem("o_split")
        mg_done = sem("merge_steps")
        mh_done = sem("merged_hi_done")
        mt_done = sem("merged_split")
        s4b_in = sem("ln1_router_in")
        tab_in = sem("tables_in")
        gate1_in = sem("gate1_in")
        mod_in = sem("shift2_scale2_in")
        bc_done = sem("mod_rows_done")
        x4_in = [sem(f"x_rows_in{i}") for i in range(2)]
        ya_done = sem("y_normed")
        x1_part = sem("x1_scaled")
        x1_done = sem("x1_done")
        x1_st = [sem(f"x1_stored{i}") for i in range(2)]
        yb_done = sem("h2_normed")
        h2_part = sem("h2_scaled")
        h2_done = sem("h2_done")
        h2t_done = sem("h2_turned_done")
        zero_done = sem("zeros_set")
        zero_st = sem("expert_rows_cleared")

        tail_no, n = {}, N_PJ + 4 * NT
        for tt in range(NT + 2):
            if tt < NT:
                tail_no["wo", tt, 0], tail_no["wo", tt, 1] = n, n + 1
                n += 2
            if tt >= 2:
                tail_no["L", tt - 2] = n
                n += 1
        for b in range(4):
            last_no[B_WA + b] = N_PJ + NT * (b + 1) - 1
        last_no[NB - 2], last_no[NB - 1] = tail_no["wo", NT - 1, 0], tail_no["wo", NT - 1, 1]
        TR_O, TR_M, TR_H = N_TR, N_TR + 2 * NT, N_TR + 3 * NT
        N_PJ2, N_TR2 = n, N_TR + 4 * NT

        def branch_block(v):
            return B_WA + v // NT
        block = ctx.enter_context(nc.Block())

        @block.sync
        def _(sp):
            for o, i in ((cond[:], t["conds"]), (ident[:], t["k_ident"]), (pick_cols[:], t["k_pick"])):
                sp.dma_start(o, i).then_inc(const_in, 16)
            def weights(b):
                for c in range(NC_CH):
                    if b:
                        sp.wait_ge(lo_done, NC_CH * (b - 1) + c + 1)
                    sp.dma_start(w_raw[:, c], block_chunk(b, c)).then_inc(raw_in[c], 16)

            weights(0)
            for tt in range(NT):
                src = t["x_prompt"][0] if tt == PROMPT else t["x_sample"][0, tt * P:(tt + 1) * P]
                sp.dma_start(x5[:, tt], src).then_inc(x_in, 16)
            for b in range(1, 4):
                weights(b)
            for i, name in enumerate(("lambda_q1", "lambda_k1", "lambda_q2", "lambda_k2")):
                sp.dma_start(lam_in[:, i], t[name][0:1, :].to_broadcast([P, HD])).then_inc(lam_in_s, 16)
            sp.dma_start(cosd[:], t["k_cos"].rearrange("(t p) d -> p t d", p=P)).then_inc(cache_in, 16)
            sp.dma_start(sind[:], t["k_sin"].rearrange("(t p) d -> p t d", p=P)).then_inc(cache_in, 16)
            sp.dma_start(nsin[:], t["k_nsin"].rearrange("(t p) d -> p t d", p=P)).then_inc(cache_in, 16)
            sp.dma_start(g_q[:], t["b_q_g"][0:1, :].to_broadcast([P, HD])).then_inc(cache_in, 16)
            sp.dma_start(g_k[:], t["b_k_g"][0:1, :].to_broadcast([P, HD])).then_inc(cache_in, 16)
            sp.dma_start(cache[:, 0:D], t["cache_a_k"][0, 0].rearrange("s h n d -> s (h n d)")).then_inc(cache_in, 16)
            sp.dma_start(cache[:, D:], t["cache_b_k"][0, 0].rearrange("s h d -> s (h d)")).then_inc(cache_in, 16)
            for b in range(4, NB - 6):
                weights(b)
            for b in range(NB - 6, NB - 4):
                weights(b)
            sp.wait_ge(pj_ready, N_PJ)
            for i in range(TST):
                sp.wait_ge(tst_st[i], tst_total[i])
            for i in range(2):
                sp.wait_ge(vst_st[i], vst_total[i])
            for bi in range(1, len(bundles)):
                if bi >= 2:
                    sp.wait_ge(s_ready, map_end[bi - 2])
                load_qk(sp, bi, qk_in[bi % 2])
                if bi >= 2:
                    sp.wait_ge(pv_ready, job_end[bi - 2])
                load_v(sp, bi, v_in[bi % 2])
            for b in range(NB - 4, NB):
                weights(b)
            sp.wait_ge(mg_done, 4 * NT)
            sp.wait_ge(pj_ready, N_PJ + 4 * NT)

            def load_x(tt):
                if tt >= 2:
                    sp.wait_ge(ya_done, tt - 1)
                src = t["x_prompt"][0] if tt == PROMPT else t["x_sample"][0, tt * P:(tt + 1) * P]
                sp.dma_start(xr[:, tt % 2], src).then_inc(x4_in[tt % 2], 16)

            for i, m in enumerate((2, 3, 4)):
                for cnd in range(2):
                    sp.dma_start(bc[:, cnd, i], mod_scr[cnd:cnd + 1, m * D:(m + 1) * D].to_broadcast([P, D])).then_inc(
                        mod_in if i else gate1_in, 16)
                if i == 0:
                    load_x(0)
            for tt in range(1, NT):
                load_x(tt)
            def block_in(q, par, half, chunk, r):
                for c in range(NC_CH):
                    dst, done, _ = landing(par, half, c)
                    sp.wait_ge(lo_done, NC_CH * (NB + q - 2) + c + 1)
                    sp.dma_start(dst, chunk(r, c)).then_inc(done, 16)

            for c in range(NC_CH):
                sp.wait_ge(lo_done, NC_CH * (NB - 1) + c + 1)
                sp.dma_start(w_raw[:, c], expert_chunk(0, 0, c)).then_inc(raw_in[c], 16)
            sp.wait_ge(pj_ready, last_no[NB - 1] + 1)
            sp.wait_ge(yb_done, NT)
            sp.wait_ge(x1_st[0], 16 * 3)
            sp.wait_ge(x1_st[1], 16 * 2)
            for c in range(NC_CH):
                sp.dma_start(raw_odd[:, c], expert_chunk(0, 1, c)).then_inc(raw2_in[c], 16)

            def tile_expert(tile):
                e = sp.value_load(ctl[0:1, bass.ds(1 + tile, 1)], min_val=0, max_val=NE - 1)
                return lambda r, c: expert_chunk(bass.ds(e, 1), r, c).rearrange("p o k n -> p (o k) n")

            sp.wait_ge(route_done, 1)
            last_pair = last_pair_of_tiles(sp)
            with sp.Fori(0, last_pair) as i:
                for s in range(2):
                    chunk = tile_expert(2 * i + 1 + s)
                    for r, (q, par, half) in enumerate(step_blocks(i, s)):
                        if r == 2:
                            chunk = tile_expert(2 * i + s)
                        block_in(q, par, half, chunk, r)
            chunk = tile_expert(2 * last_pair + 1)
            for r, (q, par, half) in enumerate(step_blocks(last_pair, 0)):
                block_in(q, par, half, tile_expert(2 * last_pair) if r == 2 else chunk, r)
            block_in(6 * last_pair + 5, 1, 3 * last_pair + 2, chunk, 2)
            sp.wait_ge(moe_over, 1)

            def load_x1(tt):
                sp.dma_start(xq[:, tt % YS], x1_scr[tt]).then_inc(x7_in[tt % YS], 16)

            for tt in range(YS):
                load_x1(tt)
            for tt in range(NT):
                s = tt % YS
                if tt + YS < NT:
                    sp.wait_ge(f_done, tt + 1)
                    load_x1(tt + YS)
                sp.wait_ge(fb_done, tt + 1)
                dst = t["y_prompt"][0] if tt == PROMPT else t["y_sample"][0, tt * P:(tt + 1) * P]
                sp.dma_start(dst, ya[:, s]).then_inc(out_st[s], 16)
            for s in range(YS):
                sp.wait_ge(out_st[s], 16 * ((NT - 1 - s) // YS + 1))

        @block.scalar
        def _(act):
            def split_hi(b):
                for c in range(NC_CH):
                    act.wait_ge(raw_in[c], 16 * (b + 1))
                    if b >= 2:
                        act.wait_ge(pj_ready, last_no[b - 2] + 1)
                    act.copy(w_hi[:, b % 2, c], w_raw[:, c]).then_inc(hi_done, 1)

            def after(i):
                kind = units[i][0]
                for j, n in zip(tst_no.get(i, []), tr_no[i]):
                    act.wait_ge(tr_ready, n + 1)
                    if j >= TST:
                        act.wait_ge(tst_st[j % TST], tst_sum[j - TST])
                    nm = B_KV if kind in ("bkv", "cbk") else 8
                    act.activation(tst[:, j % TST, 0:nm].rearrange("p m q -> p (m q)"), turned(n)[:, 0:nm * P],
                                   ACT.Copy, scale=SCALE if kind in ("q", "bq") else 1.0).then_inc(tr_free[n % 2], 1)

            def post(i):
                kind, b, ci, tt = units[i]
                if kind == "ada":
                    act.wait_ge(pj_ready, pj_no[i] + 1)
                    if ci >= 2:
                        prev = [q for q, u in enumerate(units) if u[0] == "ada" and u[2] == ci - 2][0]
                        act.wait_ge(tr_ready, tr_no[prev][0] + 1)
                    act.copy(stage5[0:4, ci % 2], bank(pj_no[i])[0:4]).then_inc(pj_free[pj_no[i] % 4], 1)
                elif kind in ("v", "g", "bkv"):
                    n, j = pj_no[i], vst_no[i]
                    act.wait_ge(pj_ready, n + 1)
                    if j >= 2:
                        act.wait_ge(vst_st[j % 2], vst_sum[j - 2])
                    if kind == "g":
                        act.activation(vst[:, j % 2], bank(n), ACT.Tanh, scale=0.5).then_inc(pj_free[n % 4], 1)
                    elif kind == "v":
                        act.copy(vst[:, j % 2], bank(n)).then_inc(pj_free[n % 4], 1)
                    else:
                        act.copy(vst[:, j % 2, 0:256], bank(n)[:, 256:512]).then_inc(v_out, 1)
                if kind in ("bq", "bkv"):
                    n = pj_no[i]
                    w = 512 if kind == "bq" else 256
                    act.wait_ge(pj_ready, n + 1)
                    k = sum(u[0] in ("bq", "bkv") for u in units[:i])
                    if k >= 2:
                        act.wait_ge(hl_done, hl_no[[q for q in range(i) if units[q][0] in ("bq", "bkv")][-2]] + 1)
                    act.activation(sq[:, k % 2, 0:w], bank(n)[:, 0:w], ACT.Square).then_inc(sq_done, 1)

            act.wait_ge(const_in, 48)
            act.activation(cond_t[:], cond[:], ACT.Tanh, scale=0.5).then_inc(cond_silu, 1)
            split_hi(0)
            for i in range(N_EARLY):
                split_hi(i + 1)
                post(i)
            for k in range(KD):
                n = H_GROUP0 + k
                act.wait_ge(tr_ready, n + 1)
                if k == 0:
                    act.wait_ge(tr_free[1], 2)
                    act.wait_ge(tr_free[0], 2)
                if k >= 2:
                    act.wait_ge(h_done, k - 1)
                act.activation(h_mod[:, k % 2, 0:N_LAT], turned(n)[:, 0:N_LAT], ACT.Identity,
                               bias=mod_t[:, k, 1:2], scale=mod_t[:, KD + k, 1:2])
                act.activation(h_mod[:, k % 2, N_LAT:], turned(n)[:, N_LAT:NT * P], ACT.Identity,
                               bias=mod_t[:, k, 0:1], scale=mod_t[:, KD + k, 0:1]).then_inc(tr_free[n % 2], 1)
            for i in range(N_EARLY, len(units)):
                if first_of_block(i):
                    split_hi(units[i][1] + 1)
                post(i)
                if i - 2 >= N_EARLY:
                    after(i - 2)
            after(len(units) - 2)
            after(len(units) - 1)
            act.wait_ge(lam_sem, 1)
            act.activation(lam_e[:], lam_s[:], ACT.Exp).then_inc(lam_sem, 1)
            for j in range(NJ + 2):
                if j < NJ:
                    for m in [m for m in range(jobs[j][4], NM) if maps[m][0] == j]:
                        act.wait_ge(nb_done, m + 1)
                        if m >= PR:
                            jl = maps[m - PR][0]
                            act.wait_ge(*((t_ready, jl + 1) if jobs[jl][1] else (a_done, jl + 1)))
                        if m >= RR:
                            act.wait_ge(o_out, maps[m - RR][0] + 1)
                        w = width(j)
                        act.activation(pbuf[:, m % PR, 0:w], spair(m)[:, 0:w], ACT.Exp, bias=nmax[:, m % RR:m % RR + 1],
                                       accum_out=rsum[:, m % RR:m % RR + 1]).then_inc(e_done, 1)
                if 2 <= j and not copied_by_dve(j - 2):
                    copy_turned(act, act.copy, j - 2)
            def load_o(z):
                if z < 2 * NT:
                    if z >= OS:
                        act.wait_ge(tr_ready, TR_O + z - OS + 1)
                    if z == NT:
                        for i in range(2):
                            act.wait_ge(o_st[i], 16 * (len(bundles) // 2))
                    tt, c0 = z % NT, (z // NT) * D
                    act.dma_start(oin[:, z % OS], o_scr[tt, :, c0:c0 + D]).then_inc(o_in[z % OS], 16)

            def square(z):
                if z < NT:
                    act.wait_ge(o_in[z % OS], 16 * (z // OS + 1))
                    if z:
                        act.wait_ge(on_done, z)
                    act.activation(sqb[:], oin[:, z % OS], ACT.Square).then_inc(osq_done, 1)

            def round_o(z):
                n = TR_O + z
                cols = slice((z % NT) * P, (z % NT + 1) * P)
                act.wait_ge(tr_ready, n + 1)
                if z == 0:
                    act.wait_ge(gcol_done, 1)
                src = turned(n)[:].rearrange("p (k q) -> p k q", q=P)
                act.activation(ot_hi[z // NT][:, :, cols], src, ACT.Copy,
                               scale=gcol[:] if z < NT else 1.0).then_inc(oh_done, 1)

            def round_merged(tt):
                n = TR_M + tt
                act.wait_ge(tr_ready, n + 1)
                act.activation(ot_hi[0][:, :, tt * P:(tt + 1) * P], turned(n)[:].rearrange("p (k q) -> p k q", q=P),
                               ACT.Copy, scale=0.5).then_inc(mh_done, 1)

            for i in range(2):
                act.wait_ge(o_st[i], 16 * (A_HEADS // 2))
            for z in range(OS):
                load_o(z)
            square(0)
            square(1)
            act.wait_ge(o_out, NJ)
            for v in range(4 * NT):
                if v < 2 * NT:
                    round_o(v)
                    load_o(v + OS)
                    square(v + 2)
                if v % NT == 0:
                    split_hi(branch_block(v) + 1)
                if v >= 3 * NT + 2:
                    round_merged(v - 3 * NT - 2)
            round_merged(NT - 2)
            round_merged(NT - 1)
            split_hi(NB - 1)
            for tt in range(NT):
                n = TR_H + tt
                act.wait_ge(tr_ready, n + 1)
                if tt:
                    act.wait_ge(pj_ready, tail_no["L", tt - 1] + 1)
                act.copy(h2t[:].rearrange("p k q -> p (k q)"), turned(n)[:]).then_inc(tr_free[n % 2], 1)
            act.wait_ge(exp_in, 1)
            act.activation(ee[:], ex[:], ACT.Exp).then_inc(exp_out, 1)
            for sm in (xh_done, th_done, ah_done, y_copied):
                act.nop().then_inc(sm, OFF)
            act.wait_ge(pj_ready, N_PJ2)

            def split_hi_moe(block):
                q, par, half = block
                for c in range(NC_CH):
                    src, done, value = landing(par, half, c)
                    act.wait_ge(done, value)
                    if not (isinstance(q, int) and q < 2):
                        act.wait_ge(moe_used, used(q - 2) + c + 1)
                    act.copy(w_hi[:, (NB + par) % 2, c], src).then_inc(hi_done, 1)

            def round_x(tile, s):
                act.wait_ge(x_turned, tile + 1 + OFF)
                act.copy(xt_hi[:, s].rearrange("p k q -> p (k q)"), pair[1][:]).then_inc(xh_done, 1)

            def gate_tanh(tile, q):
                act.wait_ge(moe_used, used(q + 1))
                act.wait_ge(hid_done, tile + OFF)
                act.activation(th[:], pair[0][:, 0:FF], ACT.Tanh, scale=0.5).then_inc(th_done, 1)

            def take_out(tile, s, q):
                act.wait_ge(moe_used, used(q + 1))
                act.wait_ge(y_free, tile - 1 + OFF)
                act.copy(yo[:, s], pair[3][:]).then_inc(y_copied, 1)

            def round_hidden(tile):
                act.wait_ge(aturned, tile + 1 + OFF)
                act.activation(at_hi[:].rearrange("p k q -> p (k q)"), pair[2][:, 0:FF], ACT.Copy,
                               scale=0.5).then_inc(ah_done, 1)

            def act_tile(i, s, final):
                tile, (gate, up, down) = 2 * i + 1 + s, step_blocks(i, s)
                split_hi_moe(down)
                gate_tanh(tile, gate[0])
                nq = 6 * i + 3 * s + 5
                if final:
                    split_hi_moe((nq, 1, 3 * i + 2))
                else:
                    split_hi_moe((nq, (3 * s + 5) % 2, 3 * i + (3 * s + 5) // 2))
                    round_x(tile + 1, s)
                    split_hi_moe((nq + 1, (3 * s + 6) % 2, 3 * i + (3 * s + 6) // 2))
                take_out(tile - 1, s, down[0])
                round_hidden(tile)

            split_hi_moe((0, 0, 0))
            split_hi_moe((1, 1, 0))
            act.wait_ge(route_done, 1)
            last_pair = last_pair_of_tiles(act)
            act.wait_ge(y_free, OFF)
            round_x(0, 0)
            split_hi_moe((2, 0, 1))
            gate_tanh(0, 0)
            split_hi_moe((3, 1, 1))
            round_x(1, 1)
            round_hidden(0)
            with act.Fori(0, last_pair) as i:
                for s in range(2):
                    act_tile(i, s, False)
            act_tile(last_pair, 0, True)
            take_out(2 * last_pair + 1, 1, 6 * last_pair + 5)
            for tt in range(NT):
                act.wait_ge(y_in[tt % YS], 32 * (tt // YS + 1))
                act.activation(ya[:, tt % YS], ya[:, tt % YS], ACT.Copy, scale=pair_w[:, tt, 0:1]).then_inc(w_first, 1)

        @block.vector
        def _(dve):
            link = chain(dve, dve_link)

            def split_lo(b):
                for c in range(NC_CH):
                    dve.wait_ge(hi_done, NC_CH * b + c + 1)
                    dve.tensor_tensor(w_lo[:, b % 2, c], w_raw[:, c], w_hi[:, b % 2, c].bitcast(F32),
                                      ALU.subtract).then_inc(lo_done, 1)

            def split_heads(i, src, nh):
                j = hl_no[i]
                if j >= 2:
                    dve.wait_ge(tr_ready, tr_no[hl_users[j - 2]][-1] + 1)
                s = src.rearrange("p (m d) -> p m d", d=HD)
                hi, lo = hl[:, j % 2, 0:nh, 0], hl[:, j % 2, 0:nh, 1]
                link(dve.tensor_copy(hi, s))
                dve.tensor_tensor(lo, s, hi.bitcast(F32), ALU.subtract).then_inc(hl_done, 1)
                dve.wait_ge(hl_done, hl_no[i] + 1)

            def rope(x, nh, tt, free):
                w = nh * HD
                xv = x.rearrange("p (m e two) -> p m e two", m=nh, two=2)
                uv = ru[:, 0:w].rearrange("p (m e two) -> p m e two", m=nh, two=2)
                xs = x.rearrange("p (m d) -> p m d", m=nh)
                dve.tensor_tensor(rt[:, 0:w].rearrange("p (m d) -> p m d", m=nh), xs,
                                  over(cosd[:, tt], 1, [P, nh, HD]), ALU.mult)
                dve.tensor_tensor(uv[:, :, :, 0], xv[:, :, :, 1], over(nsin[:, tt], 1, [P, nh, HD // 2]), ALU.mult)
                last = dve.tensor_tensor(uv[:, :, :, 1], xv[:, :, :, 0], over(sind[:, tt], 1, [P, nh, HD // 2]),
                                         ALU.mult)
                if free is None:
                    link(last)
                else:
                    sm, val = free
                    last.then_inc(sm, 1)
                    dve.wait_ge(sm, val)
                link(dve.tensor_tensor(rr[:, 0:w], rt[:, 0:w], ru[:, 0:w], ALU.add))

            def post(i):
                kind, b, ci, tt = units[i]
                if kind == "ck":
                    if ci == 0:
                        dve.wait_ge(cache_in, 112)
                    split_heads(i, cache[:, ci * CW:(ci + 1) * CW], 8)
                elif kind == "cbk":
                    split_heads(i, cache[:, D:], B_KV)
                elif kind in ("q", "k"):
                    n = pj_no[i]
                    dve.wait_ge(pj_ready, n + 1)
                    free = (pj_free[n % 4], n // 4 + 1)
                    if n == 4:
                        dve.wait_ge(cache_in, 112)
                    if tt != PROMPT:
                        rope(bank(n), 8, tt, free)
                        split_heads(i, rr[:], 8)
                    elif kind == "q":
                        dve.tensor_copy(rr[:], bank(n)).then_inc(free[0], 1)
                        dve.wait_ge(*free)
                        split_heads(i, rr[:], 8)
                    else:
                        s = pst_no[i]
                        if s >= 2:
                            dve.wait_ge(pst_st[s % 2], 16 * (s // 2))
                        dve.tensor_copy(pst[:, s % 2], bank(n)).then_inc(free[0], 1)
                        dve.wait_ge(*free)
                        split_heads(i, pst[:, s % 2], 8)
                elif kind in ("bq", "bkv"):
                    n = pj_no[i]
                    w, nh = (512, 8) if kind == "bq" else (256, 4)
                    gain = g_q if kind == "bq" else g_k
                    k = sum(u[0] in ("bq", "bkv") for u in units[:i])
                    dve.wait_ge(sq_done, k + 1)
                    s3 = "p (m d) -> p m d"
                    link(dve.tensor_reduce(ms8[:, 0:nh], sq[:, k % 2, 0:w].rearrange(s3, d=HD), AX.X, ALU.add))
                    link(dve.tensor_scalar(ms8[:, 0:nh], ms8[:, 0:nh], 1.0 / HD, EPS, ALU.mult, ALU.add))
                    rsqrt(dve, link, rs8[:, 0:nh], ms8[:, 0:nh], hf8[:, 0:nh], sh8[:, 0:nh])
                    if kind == "bkv":
                        dve.wait_ge(v_out, sum(u[0] == "bkv" for u in units[:i + 1]))
                    dve.tensor_tensor(qn[:, 0:w].rearrange(s3, d=HD), bank(n)[:, 0:w].rearrange(s3, d=HD),
                                      over(rs8[:, 0:nh], 2, [P, nh, HD]), ALU.mult).then_inc(pj_free[n % 4], 1)
                    dve.wait_ge(pj_free[n % 4], n // 4 + 1)
                    if kind == "bkv" and tt == PROMPT:
                        s = pst_no[i]
                        dve.wait_ge(pst_st[s % 2], 16 * (s // 2))
                        dst = pst[:, s % 2, 0:w]
                    else:
                        dst = qn[:, 0:w]
                    link(dve.tensor_tensor(dst.rearrange(s3, d=HD), qn[:, 0:w].rearrange(s3, d=HD),
                                           over(gain[:], 1, [P, nh, HD]), ALU.mult))
                    if tt != PROMPT:
                        rope(qn[:, 0:w], nh, tt, None)
                        split_heads(i, rr[:, 0:w], nh)
                    else:
                        split_heads(i, dst, nh)

            def after(i):
                kind, b, ci, tt = units[i]
                if kind != "ada":
                    return
                n = tr_no[i][0]
                dve.wait_ge(tr_ready, n + 1)
                if ci < 4:
                    dst = mod_t[:, 4 * ci:4 * ci + 4].rearrange("p k c -> p (k c)")
                    if ci < 2:
                        dve.tensor_copy(dst, turned(n)[:, 0:8]).then_inc(tr_free[n % 2], 1)
                    else:
                        dve.tensor_scalar(dst, turned(n)[:, 0:8], 1.0, None, ALU.add).then_inc(tr_free[n % 2], 1)
                else:
                    m = ms_no[i]
                    if m >= 2:
                        dve.wait_ge(ms_st[m % 2], 16 * (m // 2))
                    dve.tensor_copy(mst[:, m % 2], turned(n)[0:2, 0:CW]).then_inc(tr_free[n % 2], 1)

            dve.wait_ge(cond_silu, 1)
            link(dve.scalar_tensor_tensor(cond_t[:], cond_t[:], 1.0, cond[:], ALU.add, ALU.mult))
            link(dve.tensor_scalar(cond_t[:], cond_t[:], 0.5, None, ALU.mult))
            link(dve.tensor_copy(cond_hl[:, :, 0:2], cond_t[:]))
            dve.tensor_tensor(cond_hl[:, :, 2:4], cond_t[:], cond_hl[:, :, 0:2].bitcast(F32),
                              ALU.subtract).then_inc(cond_silu, 1)
            split_lo(0)
            for tt in range(NT):
                dve.wait_ge(x_in, 16 * NT)
                for h in range(2):
                    last = dve.bn_stats(stats[:, tt, 6 * h:6 * h + 6], x5[:, tt, h * CW:(h + 1) * CW])
                link(last)
                link(dve.bn_aggr(mv[:, tt], stats[:, tt]))
            link(dve.tensor_scalar(var5[:], mv[:, :, 1], EPS, None, ALU.add))
            rsqrt(dve, link, rstd5[:], var5[:], half5[:], shift5[:])
            for tt in range(NT):
                dve.tensor_scalar(x5[:, tt], x5[:, tt], mv[:, tt, 0:1], rstd5[:, tt:tt + 1],
                                  ALU.subtract, ALU.mult).then_inc(norm_done, 1)
            for i in range(N_EARLY):
                split_lo(i + 1)
                if i:
                    after(i - 1)
            after(N_EARLY - 1)
            for k in range(KD):
                dve.wait_ge(tr_free[(H_GROUP0 + k) % 2], (H_GROUP0 + k) // 2 + 1)
                link(dve.tensor_copy(h_hi[:, k], h_mod[:, k % 2]))
                dve.tensor_tensor(h_lo[:, k], h_mod[:, k % 2], h_hi[:, k].bitcast(F32),
                                  ALU.subtract).then_inc(h_done, 1)
            for i in range(N_EARLY, len(units)):
                if first_of_block(i):
                    split_lo(units[i][1] + 1)
                post(i)
                if i - 2 >= N_EARLY:
                    after(i - 2)
            after(len(units) - 2)
            after(len(units) - 1)
            dve.wait_ge(lam_in_s, 64)
            link(dve.tensor_tensor(lam_in[:, 0:4:2], lam_in[:, 0:4:2], lam_in[:, 1:4:2], ALU.mult))
            dve.tensor_reduce(lam_s[:], lam_in[:, 0:4:2], AX.X, ALU.add).then_inc(lam_sem, 1)
            dve.wait_ge(lam_sem, 2)
            link(dve.tensor_tensor(nlam[:], lam_e[:, 1:2], lam_e[:, 0:1], ALU.subtract))
            link(dve.tensor_scalar(nlam[:], nlam[:], -LAMBDA_INIT, None, ALU.add))
            for j in range(NJ + 4):
                if j < NJ:
                    for m in [m for m in range(jobs[j][4], NM) if maps[m][0] == j]:
                        dve.wait_ge(s_ready, m + 1)
                        if m >= RR:
                            dve.wait_ge(e_done, m - RR + 1)
                        dve.tensor_reduce(nmax[:, m % RR:m % RR + 1], spair(m)[:, 0:width(j)], AX.X, ALU.max,
                                          negate=True).then_inc(nb_done, 1)
                i = j - 1
                if 0 <= i < NJ and jobs[i][1] == 0:
                    m, w = jobs[i][4], width(i)
                    s0, s1_ = m % RR, m % RR + 1
                    dve.wait_ge(e_done, m + 2)
                    if i >= 2:
                        dve.wait_ge(t_ready, i - 1)
                    link(dve.reciprocal(rinv[:, s0:s0 + 2], rsum[:, s0:s0 + 2]))
                    link(dve.scalar_tensor_tensor(coef[:], rsum[:, s0:s0 + 1], nlam[:], rinv[:, s1_:s1_ + 1], ALU.mult, ALU.mult))
                    dve.scalar_tensor_tensor(abuf[:, i % 2, 0:w], pbuf[:, (m + 1) % PR, 0:w], coef[:], pbuf[:, m % PR, 0:w],
                                             ALU.mult, ALU.add).then_inc(a_done, 1)
                    dve.wait_ge(a_done, i + 1)
                i = j - 2
                if 0 <= i < NJ and copied_by_dve(i):
                    copy_turned(dve, dve.tensor_copy, i)
                i = j - 4
                if 0 <= i < NJ:
                    bi, kind, r, tt, m = jobs[i]
                    slot, w = m % RR, HD if kind else P
                    if kind:
                        link(dve.reciprocal(rinv[:, slot:slot + 1], rsum[:, slot:slot + 1]))
                    dve.wait_ge(pv_ready, i + 1)
                    if bi >= 2:
                        dve.wait_ge(o_st[bi % 2], 16 * (bi // 2))
                    dve.tensor_scalar(ost[:, bi % 2, tt, r * HD:r * HD + w], obank(i)[:, 0:w], rinv[:, slot:slot + 1], None,
                                      ALU.mult).then_inc(o_out, 1)
            def norm_o(z):
                if z >= NT:
                    return
                dve.wait_ge(osq_done, z + 1)
                link(dve.tensor_reduce(oms[:], sqb[:].rearrange("p (h d) -> p h d", d=P), AX.X, ALU.add))
                link(dve.tensor_scalar(oms[:], oms[:], 1.0 / P, EPS, ALU.mult, ALU.add))
                rsqrt(dve, link, ors[:], oms[:], ohf[:], osh[:])
                o = oin[:, z % OS].rearrange("p (h d) -> p h d", d=P)
                dve.tensor_tensor(o, o, over(ors[:], 2, [P, A_HEADS, P]), ALU.mult).then_inc(on_done, 1)
                dve.wait_ge(on_done, z + 1)

            def rest_o(z):
                n = TR_O + z
                cols = slice((z % NT) * P, (z % NT + 1) * P)
                dve.wait_ge(oh_done, z + 1)
                dve.scalar_tensor_tensor(ot_lo[z // NT][:, :, cols], turned(n)[:].rearrange("p (k q) -> p k q", q=P),
                                         gcol[:] if z < NT else 1.0, ot_hi[z // NT][:, :, cols].bitcast(F32),
                                         ALU.mult, ALU.subtract).then_inc(tr_free[n % 2], 1)

            def rest_merged(tt):
                n = TR_M + tt
                cols = slice(tt * P, (tt + 1) * P)
                dve.wait_ge(mh_done, tt + 1)
                dve.scalar_tensor_tensor(ot_lo[0][:, :, cols], turned(n)[:].rearrange("p (k q) -> p k q", q=P),
                                         0.5, ot_hi[0][:, :, cols].bitcast(F32),
                                         ALU.mult, ALU.subtract).then_inc(tr_free[n % 2], 1)

            def merge(v):
                n, tt = N_PJ + v, v % NT
                part = rows[:, tt, (v // (2 * NT)) * CW:(v // (2 * NT) + 1) * CW]
                dve.wait_ge(pj_ready, n + 1)
                dve.wait_ge(g_in[v % 2], 16 * (v // 2 + 1))
                second = (v // NT) % 2
                dve.scalar_tensor_tensor(gated[:] if second else part, gin[:, v % 2], 1.0, bank(n),
                                         ALU.add, ALU.mult).then_inc(pj_free[n % 4], 1)
                dve.wait_ge(pj_free[n % 4], n // 4 + 1)
                if second:
                    dve.tensor_tensor(part, part, gated[:], ALU.add).then_inc(mg_done, 1)
                else:
                    dve.nop().then_inc(mg_done, 1)
                dve.wait_ge(mg_done, v + 1)

            norm_o(0)
            dve.wait_ge(pv_ready, NJ)
            dve.memset(zero[:], 0.0).then_inc(zero_done, 1)
            dve.wait_ge(gcol_in, 16)
            dve.tensor_scalar(gcol[:], gcol[:], 1.0 - LAMBDA_INIT, None, ALU.mult).then_inc(gcol_done, 1)
            dve.wait_ge(gcol_done, 1)
            for v in range(4 * NT):
                if v < 2 * NT:
                    rest_o(v)
                if v:
                    merge(v - 1)
                else:
                    norm_o(1)
                if v < 2 * NT:
                    norm_o(v + 2)
                if v % NT == 0:
                    split_lo(branch_block(v) + 1)
                if v >= 3 * NT + 2:
                    rest_merged(v - 3 * NT - 2)
            merge(4 * NT - 1)
            rest_merged(NT - 2)
            rest_merged(NT - 1)
            split_lo(NB - 1)

            def row_norm(src, dst, done):
                for h in range(2):
                    last = dve.bn_stats(st4[:, 6 * h:6 * h + 6], src[:, h * CW:(h + 1) * CW])
                link(last)
                link(dve.bn_aggr(mv4[:], st4[:]))
                link(dve.tensor_scalar(va4[:], mv4[:, 1:2], EPS, None, ALU.add))
                rsqrt(dve, link, rs4[:], va4[:], hf4[:], sh4[:])
                sm, val = done
                dve.tensor_scalar(dst, src, mv4[:, 0:1], rs4[:], ALU.subtract, ALU.mult).then_inc(sm, 1)
                dve.wait_ge(sm, val)

            def first_norm(tt):
                cnd = 0 if tt == PROMPT else 1
                y = yb[:, tt % 2]
                if tt >= 2:
                    dve.wait_ge(x1_st[tt % 2], 16 * (tt // 2))
                for h in range(2):
                    n = tail_no["wo", tt, h]
                    dve.wait_ge(pj_ready, n + 1)
                    c = slice(h * CW, (h + 1) * CW)
                    dve.tensor_tensor(y[:, c], bank(n), bc[:, cnd, 0, c], ALU.mult).then_inc(pj_free[n % 4], 1)
                dve.wait_ge(pj_free[n % 4], n // 4 + 1)
                dve.wait_ge(x4_in[tt % 2], 16 * (tt // 2 + 1))
                link(dve.scalar_tensor_tensor(y, xr[:, tt % 2], ALPHA, y, ALU.mult, ALU.add))
                row_norm(y, y, (ya_done, tt + 1))

            def second_norm(tt):
                dve.wait_ge(x1_done, tt + 1)
                row_norm(yb[:, tt % 2], rows[:, tt], (yb_done, tt + 1))

            def take_logits(tt):
                n = tail_no["L", tt]
                dve.wait_ge(pj_ready, n + 1)
                dve.wait_ge(s4b_in, 6 * 16)
                dve.tensor_tensor(logit[:, tt], bank(n)[:, 0:NG + NE], b_rt[:], ALU.add).then_inc(pj_free[n % 4], 1)
                dve.wait_ge(pj_free[n % 4], n // 4 + 1)

            dve.wait_ge(gate1_in, 32)
            for tt in range(NT + 1):
                if tt < NT:
                    first_norm(tt)
                if tt == 0:
                    dve.wait_ge(mod_in, 64)
                    dve.tensor_scalar(bc[:, :, 2], bc[:, :, 2], 1.0, None, ALU.add).then_inc(bc_done, 1)
                if tt:
                    second_norm(tt - 1)
                if tt >= 2:
                    take_logits(tt - 2)
            take_logits(NT - 1)
            dve.wait_ge(h2_done, NT)
            dve.wait_ge(x1_st[0], 16 * 3)
            dve.wait_ge(x1_st[1], 16 * 2)
            dve.memset(ones[:], 1.0).then_inc(ones_done, 1)
            dve.wait_ge(tab_in, 32)
            lc, lf = logit[:, :, 0:NG], logit[:, :, NG:].rearrange("p t (g e) -> p t g e", g=NG)
            w4 = over(tab[:, T_PRI:T_PRI + NG], 1, [P, NT, NG])

            def pick_max(dst, src, top):
                link(dve.tensor_reduce(top, src, AX.X, ALU.max))
                link(dve.tensor_tensor(dst, src, over(top, 2, [P, NT, NG]), ALU.is_equal))
                link(dve.tensor_tensor(dst, dst, w4, ALU.mult))
                link(dve.tensor_reduce(pri[:], dst, AX.X, ALU.max))
                link(dve.tensor_tensor(dst, dst, over(pri[:], 2, [P, NT, NG]), ALU.is_equal))

            pick_max(oh_g[:], lc, mc[:])
            link(dve.tensor_tensor(ex[:, :, 0:NG], lc, over(mc[:], 2, [P, NT, NG]), ALU.subtract))
            link(dve.tensor_tensor(prod[:], lf, over(oh_g[:], 3, [P, NT, NG, EPG]), ALU.mult))
            link(dve.tensor_reduce(fs[:], prod[:].rearrange("p t g e -> p t e g"), AX.X, ALU.add))
            pick_max(pk[0][:], fs[:], m1[:])
            link(dve.scalar_tensor_tensor(fs[:], pk[0][:], -3.0e38, fs[:], ALU.mult, ALU.add))
            pick_max(pk[1][:], fs[:], m2[:])
            dve.tensor_tensor(ex[:, :, NG], m2[:], m1[:], ALU.subtract).then_inc(exp_in, 1)
            for i in range(2):
                link(dve.tensor_tensor(choice[i][:], over(oh_g[:], 3, [P, NT, NG, EPG]),
                                       over(pk[i][:], 2, [P, NT, NG, EPG]), ALU.mult))
            pick = [x[:].rearrange("p t g e -> p t (g e)") for x in choice]
            dve.tensor_tensor(mask[:], pick[0], pick[1], ALU.add).then_inc(mask_done, 1)
            dve.wait_ge(exp_out, 1)
            link(dve.tensor_reduce(den[:], ee[:, :, 0:NG], AX.X, ALU.add))
            link(dve.scalar_tensor_tensor(den[:], ee[:, :, NG], 1.0, den[:], ALU.add, ALU.mult))
            link(dve.reciprocal(pair_w[:, :, 0], den[:]))
            link(dve.tensor_tensor(pair_w[:, :, 1], pair_w[:, :, 0], ee[:, :, NG], ALU.mult))
            dve.wait_ge(pre_done, 1)
            tile_sum = pair[0][:, NT * NE:2 * NT * NE].rearrange("p (t e) -> p t e", e=NE)
            link(dve.tensor_copy(posn[:, 0:NT].rearrange("p t e -> p (t e)"), pair[0][:, 0:NT * NE]))
            link(dve.tensor_copy(sofar[:], tile_sum[:, 0]))
            for q in range(1, NT):
                link(dve.tensor_tensor(posn[:, q], posn[:, q], sofar[:], ALU.add))
                link(dve.tensor_tensor(sofar[:] if q < NT - 1 else posn[:, NT], sofar[:], tile_sum[:, q], ALU.add))
            cnt = posn[:, NT]
            link(dve.tensor_scalar(nov[:], cnt, float(P), None, ALU.is_gt))
            for k in range(2, NT):
                link(dve.scalar_tensor_tensor(nov[:], cnt, float(k * P), nov[:], ALU.is_gt, ALU.add))
            link(dve.tensor_tensor(tri[:], tab[:, T_TRI:T_ROW].rearrange("p (a b) -> p a b", a=NE),
                                   over(nov[:], 1, [P, NE, NE]), ALU.mult))
            link(dve.tensor_reduce(ovc[:], tri[:], AX.X, ALU.add))
            v1 = tab[:, T_ROW:T_ROW + NE]
            link(dve.tensor_tensor(v2[:], ovc[:], nov[:], ALU.subtract))
            link(dve.tensor_scalar(v2[:], v2[:], float(NE - 1), float(P), ALU.add, ALU.mult))
            link(dve.tensor_tensor(v2[:], v2[:], v1, ALU.subtract))
            pos = posn[:, 0:NT]
            p16 = prod[:].rearrange("p t g e -> p t (g e)")
            link(dve.scalar_tensor_tensor(p16, pos, float(P), over(v2[:], 1, [P, NT, NE]), ALU.is_ge, ALU.mult))
            link(dve.tensor_tensor(pos, pos, p16, ALU.add))
            link(dve.tensor_tensor(pos, pos, over(v1, 1, [P, NT, NE]), ALU.add))
            for i in range(2):
                link(dve.tensor_tensor(p16, pos, pick[i], ALU.mult))
                link(dve.tensor_reduce(slotf[:, :, i], p16, AX.X, ALU.add))
            link(dve.tensor_copy(slot_i[:], slotf[:]))
            link(dve.tensor_tensor(cle[:, 0, 0:MORE // 2], ovc[:, NE - 1:NE].to_broadcast([P, MORE // 2]),
                                   tab[:, T_PAIR:T_PAIR + MORE // 2], ALU.is_gt))
            link(dve.tensor_reduce(cf[:, 0:1], cle[:, 0, 0:MORE // 2], AX.X, ALU.add))
            link(dve.tensor_scalar(cf[:, 0:1], cf[:, 0:1], float(NE // 2 - 1), None, ALU.add))
            link(dve.tensor_copy(cf[:, 1:1 + TILES], tab[:, T_TILE:T_TILE + TILES]))
            link(dve.tensor_tensor(cle[:], over(ovc[:], 1, [P, MORE, NE]),
                                   over(tab[:, T_MORE:T_MORE + MORE], 2, [P, MORE, NE]), ALU.is_le))
            link(dve.tensor_reduce(cf[:, 1 + NE:], cle[:], AX.X, ALU.add))
            link(dve.tensor_scalar(cf[:, 1 + NE:], cf[:, 1 + NE:], float(NE - 1), None, ALU.min))
            dve.tensor_copy(ctl[:], cf[:]).then_inc(route_done, 1)
            for sm in (xl_done, silu_done, hid_done, al_done):
                dve.nop().then_inc(sm, OFF)

            def split_lo_moe(block):
                q, par, _ = block
                for c in range(NC_CH):
                    dve.wait_ge(hi_done, NC_CH * (NB + q) + c + 1)
                    dve.tensor_tensor(w_lo[:, (NB + par) % 2, c], landing(par, 0, c)[0], w_hi[:, (NB + par) % 2, c].bitcast(F32),
                                      ALU.subtract).then_inc(lo_done, 1)

            def rest_x(tile, s):
                dve.wait_ge(xh_done, tile + 1 + OFF)
                dve.tensor_tensor(xt_lo[:, s].rearrange("p k q -> p (k q)"), pair[1][:],
                                  xt_hi[:, s].rearrange("p k q -> p (k q)").bitcast(F32), ALU.subtract).then_inc(xl_done, 1)

            def silu(tile):
                dve.wait_ge(th_done, tile + 1 + OFF)
                dve.wait_ge(aturned, tile + OFF)
                dve.scalar_tensor_tensor(ac[:], th[:], 1.0, pair[0][:, 0:FF], ALU.add, ALU.mult).then_inc(silu_done, 1)

            def times_up(tile, q):
                dve.wait_ge(moe_used, used(q + 1))
                dve.wait_ge(silu_done, tile + 1 + OFF)
                dve.tensor_tensor(ac[:], ac[:], pair[0][:, FF:], ALU.mult).then_inc(hid_done, 1)

            def rest_hidden(tile):
                dve.wait_ge(ah_done, tile + 1 + OFF)
                dve.scalar_tensor_tensor(at_lo[:].rearrange("p k q -> p (k q)"), pair[2][:, 0:FF], 0.5,
                                         at_hi[:].rearrange("p k q -> p (k q)").bitcast(F32),
                                         ALU.mult, ALU.subtract).then_inc(al_done, 1)

            def dve_tile(i, s, final):
                tile, (gate, up, down) = 2 * i + 1 + s, step_blocks(i, s)
                split_lo_moe(down)
                silu(tile)
                nq = 6 * i + 3 * s + 5
                if final:
                    split_lo_moe((nq, 1, 0))
                    times_up(tile, up[0])
                else:
                    split_lo_moe((nq, (3 * s + 5) % 2, 0))
                    times_up(tile, up[0])
                    rest_x(tile + 1, s)
                    split_lo_moe((nq + 1, (3 * s + 6) % 2, 0))
                rest_hidden(tile)

            dve.wait_ge(route_done, 1)
            last_pair = last_pair_of_tiles(dve)
            split_lo_moe((0, 0, 0))
            split_lo_moe((1, 1, 0))
            rest_x(0, 0)
            split_lo_moe((2, 0, 0))
            silu(0)
            split_lo_moe((3, 1, 0))
            times_up(0, 1)
            rest_x(1, 1)
            rest_hidden(0)
            with dve.Fori(0, last_pair) as i:
                for s in range(2):
                    dve_tile(i, s, False)
            dve_tile(last_pair, 0, True)
            dve.wait_ge(s7_in, 64)
            for tt in range(NT):
                cnd = 0 if tt == PROMPT else 1
                y = ya[:, tt % YS]
                dve.wait_ge(w_first, tt + 1)
                link(dve.scalar_tensor_tensor(y, yc[:, tt % YS], pair_w[:, tt, 1:2], y, ALU.mult, ALU.add))
                link(dve.tensor_tensor(y, y, g2[:, cnd], ALU.mult))
                dve.wait_ge(x7_in[tt % YS], 16 * (tt // YS + 1))
                link(dve.scalar_tensor_tensor(y, xq[:, tt % YS], ALPHA, y, ALU.mult, ALU.add))
                row_norm(y, y, (f_done, tt + 1))

        @block.tensor
        def _(pe):
            def wait_bank(n):
                if n >= 4:
                    pe.wait_ge(pj_free[n % 4], n // 4)

            def wait_turned(n):
                if n >= 2:
                    pe.wait_ge(tr_free[n % 2], n // 2)

            def project(i):
                kind, b, ci, tt = units[i]
                if b is None:
                    return
                n = pj_no[i]
                wait_bank(n)
                if first_of_block(i):
                    pe.wait_ge(lo_done, NC_CH * (b + 1))
                for kk in range(KD):
                    hi, lo = w_hi[:, b % 2, kk // 2, kk % 2], w_lo[:, b % 2, kk // 2, kk % 2]
                    first, end = kk == 0, kk == KD - 1
                    if kind == "ada":
                        pe.matmul(bank(n)[0:4], cond_hl[:, kk], hi, start=first, stop=False)
                        last = pe.matmul(bank(n)[0:4], cond_hl[:, kk], lo, start=False, stop=end)
                    else:
                        a_hi, a_lo = h_hi[:, kk, tt * P:(tt + 1) * P], h_lo[:, kk, tt * P:(tt + 1) * P]
                        pe.matmul(bank(n), a_hi, hi, start=first, stop=False)
                        pe.matmul(bank(n), a_hi, lo, start=False, stop=False)
                        last = pe.matmul(bank(n), a_lo, hi, start=False, stop=end)
                last.then_inc(pj_ready, 1)

            def turn(i):
                kind, b, ci, tt = units[i]
                if kind == "ada":
                    n = tr_no[i][0]
                    wait_turned(n)
                    pe.wait_ge(pj_free[pj_no[i] % 4], pj_no[i] // 4 + 1)
                    pe.wait_ge(stage5_in[ci % 2], 16 * (ci // 2 + 1))
                    if ci < 4:
                        for j in range(4):
                            last = pe.matmul(turned(n)[:, 2 * j:2 * j + 2], stage5[:, ci % 2, j * P:(j + 1) * P],
                                             pick_cols[:], start=j == 0, stop=True, skip_group_check=True)
                    else:
                        last = pe.matmul(turned(n)[0:2, 0:CW], pick_cols[:], stage5[:, ci % 2], start=True, stop=True)
                    last.then_inc(tr_ready, 1)
                    return
                if i not in hl_no:
                    return
                s = hl_no[i] % 2
                pe.wait_ge(hl_done, hl_no[i] + 1)
                n = tr_no[i][0]
                wait_turned(n)
                for m in range(B_KV if kind in ("bkv", "cbk") else 8):
                    src = hl[:, s, m].rearrange("p h d -> p (h d)")
                    last = pe.transpose(turned(n)[:, m * P:(m + 1) * P], src.bitcast(F32), ident[:])
                last.then_inc(tr_ready, 1)

            pe.wait_ge(cond_silu, 2)
            pe.wait_ge(const_in, 48)
            for i in range(N_EARLY):
                project(i)
                if i:
                    turn(i - 1)
            turn(N_EARLY - 1)
            pe.wait_ge(norm_done, NT)
            for k in range(KD):
                n = H_GROUP0 + k
                wait_turned(n)
                for tt in range(NT):
                    last = pe.transpose(turned(n)[:, tt * P:(tt + 1) * P], x5[:, tt, k * P:(k + 1) * P], ident[:])
                last.then_inc(tr_ready, 1)
            pe.wait_ge(h_done, KD)
            for i in range(N_EARLY, len(units)):
                project(i)
                if i - 2 >= N_EARLY:
                    turn(i - 2)
            turn(len(units) - 2)
            turn(len(units) - 1)
            for i in range(4):
                pe.wait_ge(pj_free[i], (N_PJ + 3 - i) // 4)
            for i in range(2):
                pe.wait_ge(tr_free[i], (N_TR + 1 - i) // 2)

            def scores(m):
                j, n = maps[m]
                bi, kind, r, tt, _ = jobs[j]
                s = bi % 2
                pe.wait_ge(*((qk_in[s], 80 * ((bi + 1) // 2)) if bi else (first_in, 112)))
                if m >= 2:
                    pe.wait_ge(e_done, m - 1)
                q = qtb[s][:, r if kind else n, tt * P:(tt + 1) * P]
                k = ktb[s][:, 0 if kind else n]
                runs = [(NKEY, 0, P)] if tt == PROMPT else [(0, 0, CW), (CW, CW, P)]
                for g in range(2):
                    for k0, c0, w in runs:
                        last = pe.matmul(spair(m)[:, c0:c0 + w], q, k[:, g, k0:k0 + w], start=g == 0, stop=g == 1)
                last.then_inc(s_ready, 1)

            def turn_p(j):
                bi, kind, r, tt, m = jobs[j]
                pe.wait_ge(*((e_done, m + 1) if kind else (a_done, j + 1)))
                if j:
                    pe.wait_ge(pt_full[(j - 1) % 2], (j - 1) // 2 + 1)
                src = pbuf[:, m % PR] if kind else abuf[:, j % 2]
                for k in range(width(j) // P):
                    last = pe.transpose(pair[2][:, k * P:(k + 1) * P], src[:, k * P:(k + 1) * P], ident[:])
                last.then_inc(t_ready, 1)

            def times_v(j):
                bi, kind, r, tt, m = jobs[j]
                pe.wait_ge(pt_full[j % 2], j // 2 + 1)
                if bi:
                    pe.wait_ge(v_in[bi % 2], 32 * ((bi + 1) // 2))
                if j >= 2:
                    pe.wait_ge(o_out, j - 1)
                tiles = [PROMPT] if tt == PROMPT else list(range(TL)) + [NT]
                w = HD if kind else P
                for k, vt in enumerate(tiles):
                    last = pe.matmul(obank(j)[:, 0:w], ptb[:, j % 2, k], vb[bi % 2][:, vt, 0:w], start=k == 0, stop=k == len(tiles) - 1)
                last.then_inc(pv_ready, 1)

            for j in range(NJ + 3):
                if j < NJ:
                    scores(jobs[j][4])
                if 0 <= j - 2 < NJ:
                    turn_p(j - 2)
                if j < NJ and not jobs[j][1]:
                    scores(jobs[j][4] + 1)
                if 0 <= j - 3 < NJ:
                    times_v(j - 3)
            pe.wait_ge(o_out, NJ)
            pe.wait_ge(e_done, NM)

            def turn_rows(n, src):
                wait_turned(n)
                for k in range(KD):
                    last = pe.transpose(turned(n)[:, k * P:(k + 1) * P], src[:, k * P:(k + 1) * P], ident[:])
                last.then_inc(tr_ready, 1)

            def turn_o(z):
                if z >= 2 * NT:
                    return
                if z < NT:
                    pe.wait_ge(on_done, z + 1)
                else:
                    pe.wait_ge(o_in[z % OS], 16 * (z // OS + 1))
                turn_rows(TR_O + z, oin[:, z % OS])

            def turn_merged(tt):
                pe.wait_ge(mg_done, 3 * NT + tt + 1)
                turn_rows(TR_M + tt, rows[:, tt])

            def three_passes(out, a_hi, a_lo, b, nk):
                for kk in range(nk):
                    hi, lo = w_hi[:, b % 2, kk // 2, kk % 2], w_lo[:, b % 2, kk // 2, kk % 2]
                    pe.matmul(out, a_hi[:, kk], hi, start=kk == 0, stop=False)
                    pe.matmul(out, a_hi[:, kk], lo, start=False, stop=False)
                    last = pe.matmul(out, a_lo[:, kk], hi, start=False, stop=kk == nk - 1)
                return last

            turn_o(0)
            for v in range(4 * NT):
                n, tt, b, br = N_PJ + v, v % NT, branch_block(v), (v // NT) % 2
                if v:
                    turn_o(v + 1)
                wait_bank(n)
                pe.wait_ge(lo_done, NC_CH * (b + 1))
                if v < 2 * NT:
                    pe.wait_ge(tr_free[(TR_O + v) % 2], (TR_O + v) // 2 + 1)
                cols = slice(tt * P, (tt + 1) * P)
                three_passes(bank(n), ot_hi[br][:, :, cols], ot_lo[br][:, :, cols], b, KD).then_inc(pj_ready, 1)
                if v == 0:
                    turn_o(1)
                if v >= 3 * NT + 1:
                    turn_merged(v - 3 * NT - 1)
            turn_merged(NT - 1)
            for tt in range(NT + 2):
                if tt < NT:
                    for h in range(2):
                        n = tail_no["wo", tt, h]
                        b = NB - 2 + h
                        wait_bank(n)
                        pe.wait_ge(lo_done, NC_CH * (b + 1))
                        pe.wait_ge(tr_free[(TR_M + tt) % 2], (TR_M + tt) // 2 + 1)
                        cols = slice(tt * P, (tt + 1) * P)
                        three_passes(bank(n), ot_hi[0][:, :, cols], ot_lo[0][:, :, cols], b, KD).then_inc(pj_ready, 1)
                if tt >= 2:
                    q = tt - 2
                    pe.wait_ge(s4b_in, 6 * 16)
                    pe.wait_ge(h2_done, q + 1)
                    turn_rows(TR_H + q, rows[:, q])
                    n = tail_no["L", q]
                    wait_bank(n)
                    pe.wait_ge(tr_free[(TR_H + q) % 2], (TR_H + q) // 2 + 1)
                    for k in range(KD):
                        last = pe.matmul(bank(n)[:, 0:NG + NE], h2t[:, k], w_rt[:, k], start=k == 0, stop=k == KD - 1)
                    last.then_inc(pj_ready, 1)
            pe.wait_ge(mask_done, 1)
            pe.wait_ge(ones_done, 1)
            pe.wait_ge(tab_in, 32)
            for i in range(4):
                pe.wait_ge(pj_free[i], (N_PJ2 + 3 - i) // 4)
            for i in range(2):
                pe.wait_ge(tr_free[i], (N_TR2 + 1 - i) // 2)
            for i, left in enumerate((before, ones)):
                last = pe.matmul(pair[0][:, i * NT * NE:(i + 1) * NT * NE], left[:], mask[:].rearrange("p t e -> p (t e)"),
                                 start=True, stop=True)
            last.then_inc(pre_done, 1)
            for sm in (x_turned, moe_used, aturned):
                pe.nop().then_inc(sm, OFF)

            def turn_x(tile, s, landed):
                pe.wait_ge(xs_in[s], landed)
                for k in range(KD):
                    last = pe.transpose(pair[1][:, k * P:(k + 1) * P], xs[:, s, k * P:(k + 1) * P], ident[:])
                last.then_inc(x_turned, 1)

            def gate_up(tile, s, blks):
                for r, (q, par, _) in enumerate(blks):
                    if r == 0:
                        pe.wait_ge(xl_done, tile + 1 + OFF)
                        pe.wait_ge(hid_done, tile + OFF)
                    out = pair[0][:, r * FF:(r + 1) * FF]
                    for c in range(NC_CH):
                        pe.wait_ge(lo_done, NC_CH * (NB + q) + c + 1)
                        for k in range(2):
                            kk = 2 * c + k
                            hi, lo = w_hi[:, (NB + par) % 2, c, k], w_lo[:, (NB + par) % 2, c, k]
                            pe.matmul(out, xt_hi[:, s, kk], hi, start=kk == 0, stop=False)
                            pe.matmul(out, xt_hi[:, s, kk], lo, start=False, stop=False)
                            last = pe.matmul(out, xt_lo[:, s, kk], hi, start=False, stop=kk == KD - 1)
                        last.then_inc(moe_used, 1)

            def down(tile, blk):
                q, par, _ = blk
                pe.wait_ge(al_done, tile + 1 + OFF)
                pe.wait_ge(y_copied, tile + OFF)
                for c in range(NC_CH):
                    pe.wait_ge(lo_done, NC_CH * (NB + q) + c + 1)
                    out = pair[3][:, (c // 2) * CW:(c // 2 + 1) * CW]
                    for k in range(2):
                        kk = 2 * (c % 2) + k
                        hi, lo = w_hi[:, (NB + par) % 2, c, k], w_lo[:, (NB + par) % 2, c, k]
                        pe.matmul(out, at_hi[:, kk], hi, start=kk == 0, stop=False)
                        pe.matmul(out, at_hi[:, kk], lo, start=False, stop=False)
                        last = pe.matmul(out, at_lo[:, kk], hi, start=False, stop=kk == KF - 1)
                    last.then_inc(moe_used, 1)

            def turn_hidden(tile):
                pe.wait_ge(hid_done, tile + 1 + OFF)
                for k in range(KF):
                    last = pe.transpose(pair[2][:, k * P:(k + 1) * P], ac[:, k * P:(k + 1) * P], ident[:])
                last.then_inc(aturned, 1)

            def pe_tile(i, s, final):
                tile, (gate, up, before_down) = 2 * i + 1 + s, step_blocks(i, s)
                gate_up(tile, 1 - s, (gate, up))
                if not final:
                    turn_x(tile + 1, s, 16 * (i + 2))
                down(tile - 1, before_down)
                turn_hidden(tile)

            pe.wait_ge(route_done, 1)
            last_pair = last_pair_of_tiles(pe)
            turn_x(0, 0, 16)
            gate_up(0, 0, ((0, 0, 0), (1, 1, 0)))
            turn_x(1, 1, 16)
            turn_hidden(0)
            with pe.Fori(0, last_pair) as i:
                for s in range(2):
                    pe_tile(i, s, False)
            pe_tile(last_pair, 0, True)
            down(2 * last_pair + 1, (6 * last_pair + 5, 1, 0))

        @block.gpsimd
        def _(pool):
            def bias(ci):
                if ci >= 2:
                    prev = [q for q, u in enumerate(units) if u[0] == "ada" and u[2] == ci - 2][0]
                    pool.wait_ge(tr_ready, tr_no[prev][0] + 1)
                pool.dma_start(stage5[4:5, ci % 2], t["b_ada"][0:1, ci * CW:(ci + 1) * CW]).then_inc(stage5_in[ci % 2], 16)

            def store_values(i):
                kind, b, ci, tt = units[i]
                n, j = pj_no[i], vst_no[i]
                if kind == "bkv":
                    pool.wait_ge(v_out, sum(u[0] == "bkv" for u in units[:i + 1]))
                else:
                    pool.wait_ge(pj_free[n % 4], n // 4 + 1)
                s, st = vst[:, j % 2], vst_st[j % 2]
                if kind == "g":
                    pool.dma_start(gate_scr[tt, :, (ci - 9) * CW:(ci - 8) * CW], s).then_inc(st, 16)
                elif kind == "v":
                    c0 = (ci - 4) * CW
                    pool.dma_start(va_scr[:, tt, c0:c0 + CW], s).then_inc(st, 16)
                    if tt == PROMPT:
                        pool.dma_start(t["new_a_v"][0, 0].rearrange("s h d -> s (h d)")[:, c0:c0 + CW],
                                       s).then_inc(st, 16)
                else:
                    pool.dma_start(vb_scr[:, tt], s[:, 0:256]).then_inc(st, 16)
                    if tt == PROMPT:
                        pool.dma_start(t["new_b_v"][0, 0].rearrange("s h d -> s (h d)"), s[:, 0:256]).then_inc(st, 16)

            def store_prompt_k(i):
                kind, b, ci, tt = units[i]
                s = pst_no[i]
                if kind == "k":
                    pool.wait_ge(pj_free[pj_no[i] % 4], pj_no[i] // 4 + 1)
                    dst = t["new_a_k"][0, 0].rearrange("s h n d -> s (h n d)")[:, (ci - 2) * CW:(ci - 1) * CW]
                    pool.dma_start(dst, pst[:, s % 2]).then_inc(pst_st[s % 2], 16)
                else:
                    pool.wait_ge(hl_done, hl_no[i] + 1)
                    pool.dma_start(t["new_b_k"][0, 0].rearrange("s h d -> s (h d)"),
                                   pst[:, s % 2, 0:256]).then_inc(pst_st[s % 2], 16)

            def store_turned(i):
                kind, b, ci, tt = units[i]
                j, n = tst_no[i][0], tr_no[i][0]
                pool.wait_ge(tr_free[n % 2], n // 2 + 1)
                st = tst_st[j % TST]
                if kind in ("q", "bq"):
                    m0, nm = (8 * ci if kind == "q" else MAPS_A + 8 * (ci - 6)), 8
                    dst = q_scr[m0:m0 + nm, :, tt * P:(tt + 1) * P]
                else:
                    m0, nm = {"k": (8 * (ci - 2), 8), "ck": (8 * ci, 8)}.get(kind, (MAPS_A, B_KV))
                    dst = k_scr[m0:m0 + nm, :, key_col(tt):key_col(tt) + P]
                pool.dma_start(dst.rearrange("m p q -> p m q"), tst[:, j % TST, 0:nm]).then_inc(st, 16)

            def after(i):
                kind, b, ci, tt = units[i]
                if i in tst_no:
                    store_turned(i)
                if i in ms_no:
                    n, m = tr_no[i][0], ms_no[i]
                    pool.wait_ge(tr_free[n % 2], n // 2 + 1)
                    pool.dma_start(mod_scr[:, ci * CW:(ci + 1) * CW], mst[:, m % 2]).then_inc(ms_st[m % 2], 16)
                if kind == "ada" and ci + 2 < 12:
                    bias(ci + 2)

            bias(0)
            bias(1)
            for i in range(N_EARLY):
                after(i)
            first_g = [i for i, u in enumerate(units) if u[0] == "g"][0]
            for i in range(N_EARLY, len(units)):
                if i == first_g:
                    for s in range(2):
                        pool.wait_ge(vst_st[s], max(vst_sum[j] for q, j in vst_no.items() if q < i and j % 2 == s))
                if i in vst_no:
                    store_values(i)
                if i in pst_no:
                    store_prompt_k(i)
                if i - 2 >= N_EARLY:
                    after(i - 2)
                if i == first_g + 2:
                    for s in range(TST):
                        pool.wait_ge(tst_st[s], tst_total[s])
                    load_qk(pool, 0, first_in)
                    load_v(pool, 0, first_in)
            after(len(units) - 2)
            after(len(units) - 1)
            pool.wait_ge(pj_ready, N_PJ)
            pool.wait_ge(h_done, KD)
            for i in range(TST):
                pool.wait_ge(tst_st[i], tst_total[i])
            for i in range(2):
                pool.wait_ge(vst_st[i], vst_total[i])
                pool.wait_ge(pst_st[i], 16 * ((N_PST + 1 - i) // 2))
                pool.wait_ge(ms_st[i], 16 * (N_MS // 2))
            for bi, (kind, h) in enumerate(bundles):
                pool.wait_ge(o_out, job_end[bi])
                c0, w = (D + 2 * P * h, 2 * P) if kind else (P * h, P)
                pool.dma_start(o_scr[:, :, c0:c0 + w].rearrange("t p c -> p t c"), ost[:, bi % 2, :, 0:w]).then_inc(o_st[bi % 2], 16)
            for i in range(2):
                pool.wait_ge(o_st[i], 16 * (len(bundles) // 2))
            pool.dma_start(gcol[:], t["a_subln_g"][0].rearrange("(d o) -> d o", o=1)).then_inc(gcol_in, 16)

            def load_gate(v):
                if v >= 2:
                    pool.wait_ge(mg_done, v - 1)
                c0 = (v // NT % 2) * D + (v // (2 * NT)) * CW
                pool.dma_start(gin[:, v % 2], gate_scr[v % NT, :, c0:c0 + CW]).then_inc(g_in[v % 2], 16)

            load_gate(0)
            load_gate(1)
            pool.dma_start(before[:], t["k_before"]).then_inc(tab_in, 16)
            pool.dma_start(tab[:], t["k_tab"][0:1, :].to_broadcast([P, TAB_W])).then_inc(tab_in, 16)
            for v in range(4 * NT - 2):
                load_gate(v + 2)
                if v == 0:
                    pool.wait_ge(zero_done, 1)
                for i in range(2 * v, min(2 * v + 2, TILES + 1)):
                    pool.dma_start(slots_scr[i * P:(i + 1) * P].rearrange("p (k c) -> p k c", c=P), over(zero[:], 1, [P, KD, P])).then_inc(zero_st, 16)
            pool.wait_ge(mg_done, 4 * NT)
            pool.wait_ge(pj_ready, N_PJ + 4 * NT)
            for i in range(2):
                pool.dma_start(ln1[:, i], t["ln1_b" if i else "ln1_g"][0:1, :].to_broadcast([P, D])).then_inc(s4b_in, 16)
            for w, b, c0, c1 in (("w_coarse", "b_coarse", 0, NG), ("w_fine", "b_fine", NG, NG + NE)):
                pool.dma_start(w_rt[:, :, c0:c1], t[w][0].rearrange("(k p) n -> p k n", p=P)).then_inc(s4b_in, 16)
                pool.dma_start(b_rt[:, c0:c1], t[b][0:1, :].to_broadcast([P, c1 - c0])).then_inc(s4b_in, 16)

            pool.wait_ge(s4b_in, 6 * 16)
            for tt in range(NT + 1):
                if tt < NT:
                    pool.wait_ge(ya_done, tt + 1)
                    y = yb[:, tt % 2]
                    pool.tensor_tensor(y, y, ln1[:, 0], ALU.mult).then_inc(x1_part, 1)
                    pool.wait_ge(x1_part, tt + 1)
                    pool.tensor_tensor(y, y, ln1[:, 1], ALU.add).then_inc(x1_done, 1)
                    pool.wait_ge(x1_done, tt + 1)
                    pool.dma_start(x1_scr[tt], y).then_inc(x1_st[tt % 2], 16)
                if tt:
                    q = tt - 1
                    cnd = 0 if q == PROMPT else 1
                    pool.wait_ge(yb_done, q + 1)
                    pool.wait_ge(bc_done, 1)
                    pool.tensor_tensor(rows[:, q], rows[:, q], bc[:, cnd, 2], ALU.mult).then_inc(h2_part, 1)
                    pool.wait_ge(h2_part, q + 1)
                    pool.tensor_tensor(rows[:, q], rows[:, q], bc[:, cnd, 1], ALU.add).then_inc(h2_done, 1)
            pool.wait_ge(x1_st[0], 48)
            pool.wait_ge(x1_st[1], 32)
            pool.wait_ge(route_done, 1)
            pool.wait_ge(zero_st, 16 * (TILES + 1))
            for tt in range(NT):
                for c in range(2):
                    pool.indirect_dma_start(out=slots_scr, out_offset=bass.IndirectOffsetOnAxis(ap=slot_i[:, tt, c:c + 1], axis=0),
                                            in_=rows[:, tt], in_offset=None).then_inc(scat_st, 16)
            last_pair = last_pair_of_tiles(pool)
            pool.nop().then_inc(y_free, OFF)
            pool.wait_ge(scat_st, 16 * 2 * NT)
            slot_tiles = slots_scr.rearrange("(n p) c -> n p c", p=P)
            pool.dma_start(xs[:, 0], slot_tiles[0]).then_inc(xs_in[0], 16)
            pool.dma_start(xs[:, 1], slot_tiles[1]).then_inc(xs_in[1], 16)
            for c in range(2):
                pool.dma_start(g2[:, c], mod_scr[c:c + 1, 5 * D:6 * D].to_broadcast([P, D])).then_inc(s7_in, 16)
                pool.dma_start(ln2[:, c], t["ln2_b" if c else "ln2_g"][0:1, :].to_broadcast([P, D])).then_inc(s7_in, 16)

            def load_rows(tile, s):
                pool.wait_ge(x_turned, tile - 1 + OFF)
                pool.dma_start(xs[:, s], slot_tiles[bass.ds(tile, 1)].rearrange("o p c -> (o p) c")).then_inc(xs_in[s], 16)

            def store_rows(tile, s, half):
                pool.wait_ge(y_copied, tile + 1 + OFF)
                pool.dma_start(slot_tiles[bass.ds(tile, 1)].rearrange("o p c -> (o p) c"), yo[:, s]).then_inc(y_st[s], 16)
                pool.wait_ge(y_st[s], 16 * (half + 1))
                pool.nop().then_inc(y_free, 1)

            load_rows(2, 0)
            with pool.Fori(0, last_pair) as i:
                for s in range(2):
                    load_rows(2 * i + 3 + s, 1 - s)
                    store_rows(2 * i + s, s, i)
            store_rows(2 * last_pair, 0, last_pair)
            store_rows(2 * last_pair + 1, 1, last_pair)
            pool.wait_ge(xs_in[0], 16 * (last_pair + 2))
            pool.nop().then_inc(y_free, 1)
            pool.nop().then_inc(moe_over, 1)

            def gather(tt):
                s = tt % YS
                for c, dst in enumerate((ya, yc)):
                    pool.indirect_dma_start(out=dst[:, s], out_offset=None, in_=slots_scr,
                                            in_offset=bass.IndirectOffsetOnAxis(ap=slot_i[:, tt, c:c + 1], axis=0)).then_inc(y_in[s], 16)

            for tt in range(YS):
                gather(tt)
            pool.wait_ge(s7_in, 64)
            for tt in range(NT):
                y = ya[:, tt % YS]
                pool.wait_ge(f_done, tt + 1)
                pool.tensor_tensor(y, y, ln2[:, 0], ALU.mult).then_inc(fg_done, 1)
                pool.wait_ge(fg_done, tt + 1)
                pool.tensor_tensor(y, y, ln2[:, 1], ALU.add).then_inc(fb_done, 1)
                if tt >= 1 and tt - 1 + YS < NT:
                    pool.wait_ge(out_st[(tt - 1) % YS], 16 * ((tt - 1) // YS + 1))
                    gather(tt - 1 + YS)
            for s in range(2):
                pool.wait_ge(vst_st[s], vst_total[s])
                pool.wait_ge(ms_st[s], 16 * (N_MS // 2))
                pool.wait_ge(pst_st[s], 16 * ((N_PST + 1 - s) // 2))


_INS = ["x_prompt", "x_sample", "cache_a_k", "cache_a_v", "cache_b_k", "cache_b_v", "w_ada", "b_ada",
        "w_in", "lambda_q1", "lambda_k1", "lambda_q2", "lambda_k2", "a_subln_g", "b_q_g", "b_k_g", "w_br_a", "w_br_b",
        "w_o", "ln1_g", "ln1_b", "w_coarse", "b_coarse", "w_fine", "b_fine", "w_gate_up", "w_down", "ln2_g", "ln2_b"]
_OUTS = [("y_prompt", (1, N_CTX, D)), ("y_sample", (1, N_LAT, D)), ("new_a_k", (1, 1, N_CTX, A_HEADS, 2, HD)),
         ("new_a_v", (1, 1, N_CTX, A_HEADS, 2 * HD)), ("new_b_k", (1, 1, N_CTX, B_KV, HD)),
         ("new_b_v", (1, 1, N_CTX, B_KV, HD))]


def shape_constants():
    f = np.float32
    half = HD // 2
    freqs = (f(10000.0) ** (-np.arange(0, half, 2, dtype=f) / f(half))).astype(f)
    rows = np.repeat(np.arange(N_LAT // GRID_W, dtype=f), GRID_W)
    cols = np.tile(np.arange(GRID_W, dtype=f), N_LAT // GRID_W)
    ang = np.concatenate([rows[:, None] * freqs, cols[:, None] * freqs], -1).astype(f)
    pick = np.array([[1, 0], [0, 1], [1, 0], [0, 1], [1, 1]], f)
    return {
        "k_ident": np.eye(P, dtype=f),
        "k_pick": pick,
        "k_cos": np.repeat(np.cos(ang).astype(f), 2, axis=1),
        "k_sin": np.sin(ang).astype(f),
        "k_nsin": (-np.sin(ang)).astype(f),
        "k_before": np.triu(np.ones((P, P), f), 1),
        "k_tab": np.concatenate([np.tril(np.ones((NE, NE), f)).ravel(), P * np.arange(NE, dtype=f), f([4, 3, 2, 1]),
                                 2 * np.arange(MORE // 2, dtype=f), np.arange(TILES, dtype=f),
                                 np.arange(MORE, dtype=f)]).reshape(1, TAB_W),
    }


def kernel(**inputs):
    import concourse.bacc as bacc
    from concourse.bass_utils import run_bass_kernel_spmd

    nc = bacc.Bacc("TRN2", target_bir_lowering=False, num_devices=1)
    arrays, t = {}, {}
    for name in _INS:
        arrays[f"in_{name}"] = np.ascontiguousarray(inputs[name])
    conds = np.stack([np.asarray(inputs["c_ctx"]), np.asarray(inputs["c"])[0]], axis=-1)
    arrays["in_conds"] = np.ascontiguousarray(conds.reshape(KD, P, 2).transpose(1, 0, 2))
    for name, a in shape_constants().items():
        arrays[f"in_{name}"] = np.ascontiguousarray(a)
    for name, a in arrays.items():
        t[name[3:]] = nc.dram_tensor(name, a.shape, mybir.dt.from_np(a.dtype), kind="ExternalInput").ap()
    for name, shape in _OUTS:
        t[name] = nc.dram_tensor(f"out_{name}", shape, F32, kind="ExternalOutput").ap()
    hybrid_step(nc, t)
    r = run_bass_kernel_spmd(nc, [arrays], core_ids=[0])
    return tuple(r.results[0][f"out_{name}"] for name, _ in _OUTS)
```
